# Optimizing a Trainium2 kernel written in Bass

```python
import math
import jax, jax.numpy as jnp
from jax import lax
import numpy as np

D_MODEL = 1024
BATCH = 1
SEQ = 512
DEPTH = 1

N_META = 16
BLOCK = 128
WINDOW = 128
PAD_FRONT = BLOCK - N_META

ATTN_HEADS = 8
ATTN_KV_HEADS = 2
HEAD_DIM = 64
ROPE_THETA = 10000.0
ATTN_Q_W = ATTN_HEADS * HEAD_DIM
ATTN_KV_W = ATTN_KV_HEADS * HEAD_DIM

GLA_HEADS = 4
GLA_KEY_DIM = 64
GLA_VAL_DIM = 128
GLA_K_W = GLA_HEADS * GLA_KEY_DIM
GLA_V_W = GLA_HEADS * GLA_VAL_DIM
GLA_GATE_RANK = 16
GLA_GATE_NORM = 16.0
GLA_CHUNK = 64

N_GROUPS = 4
EXPERTS_PER_GROUP = 8
EXPERT_TOP_K = 2
EXPERT_FF = 256

NORM_EPS = 1e-6
MASK_VALUE = -1e30

IN_WIDTHS = (ATTN_Q_W, ATTN_KV_W, ATTN_KV_W,
             GLA_K_W, GLA_K_W, GLA_V_W, GLA_V_W,
             GLA_GATE_RANK,
             D_MODEL, D_MODEL)
IN_TOTAL = sum(IN_WIDTHS)

kernel_name = "hybrid_swa_sink_gla_hmoe_meta"

def rms_norm(x, w):
    xf = x.astype(jnp.float32)
    y = xf * lax.rsqrt(jnp.mean(xf * xf, axis=-1, keepdims=True) + NORM_EPS)
    return (y * w.astype(jnp.float32)).astype(x.dtype)

def rope(x, pos):
    half = HEAD_DIM // 2
    inv_freq = ROPE_THETA ** (-(jnp.arange(half, dtype=jnp.float32) * 2.0) / HEAD_DIM)
    ang = pos.astype(jnp.float32)[:, None] * inv_freq[None, :]
    cos = jnp.cos(ang)[None, :, None, :]
    sin = jnp.sin(ang)[None, :, None, :]
    xf = x.astype(jnp.float32)
    x1, x2 = xf[..., :half], xf[..., half:]
    return jnp.concatenate([x1 * cos - x2 * sin, x2 * cos + x1 * sin], axis=-1).astype(x.dtype)

def swa_with_sinks(q, k, v, sinks):
    B, T = q.shape[0], q.shape[1]
    nb = T // BLOCK
    G = ATTN_HEADS // ATTN_KV_HEADS
    qb = q.reshape(B, nb, BLOCK, ATTN_KV_HEADS, G, HEAD_DIM)
    kb = k.reshape(B, nb, BLOCK, ATTN_KV_HEADS, HEAD_DIM)
    vb = v.reshape(B, nb, BLOCK, ATTN_KV_HEADS, HEAD_DIM)
    pad5 = ((0, 0), (1, 0), (0, 0), (0, 0), (0, 0))
    k_band = jnp.concatenate([jnp.pad(kb, pad5)[:, :-1], kb], axis=2)
    v_band = jnp.concatenate([jnp.pad(vb, pad5)[:, :-1], vb], axis=2)
    k_meta = k[:, PAD_FRONT:BLOCK]
    v_meta = v[:, PAD_FRONT:BLOCK]
    scale = 1.0 / math.sqrt(HEAD_DIM)
    s_band = jnp.einsum('bnqhgd,bnkhd->bnhgqk', qb, k_band).astype(jnp.float32) * scale
    s_meta = jnp.einsum('bnqhgd,bmhd->bnhgqm', qb, k_meta).astype(jnp.float32) * scale
    q_idx = jnp.arange(nb)[:, None] * BLOCK + jnp.arange(BLOCK)[None, :]
    k_idx = (jnp.arange(nb)[:, None] - 1) * BLOCK + jnp.arange(2 * BLOCK)[None, :]
    dq = q_idx[:, :, None] - k_idx[:, None, :]
    band_ok = (dq >= 0) & (dq < WINDOW) & (k_idx[:, None, :] >= BLOCK)
    meta_idx = PAD_FRONT + jnp.arange(N_META)
    meta_ok = meta_idx[None, None, :] <= q_idx[:, :, None]
    s_band = jnp.where(band_ok[None, :, None, None], s_band, MASK_VALUE)
    s_meta = jnp.where(meta_ok[None, :, None, None], s_meta, MASK_VALUE)
    sink = jnp.broadcast_to(sinks.astype(jnp.float32).reshape(1, 1, ATTN_KV_HEADS, G, 1, 1),
                            s_meta.shape[:-1] + (1,))
    p = jax.nn.softmax(jnp.concatenate([s_meta, s_band, sink], axis=-1), axis=-1)
    p_meta = p[..., :N_META].astype(v.dtype)
    p_band = p[..., N_META:N_META + 2 * BLOCK].astype(v.dtype)
    o = (jnp.einsum('bnhgqk,bnkhd->bnqhgd', p_band, v_band)
         + jnp.einsum('bnhgqm,bmhd->bnqhgd', p_meta, v_meta))
    return o.reshape(B, T, ATTN_Q_W)

def gla_chunked(q, k, v, gk):
    B, T, H, DK = q.shape
    DV = v.shape[-1]
    n = T // GLA_CHUNK
    def chunks(a):
        return a.astype(jnp.float32).reshape(B, n, GLA_CHUNK, H, a.shape[-1]).transpose(0, 3, 1, 2, 4)
    qc = chunks(q) * (DK ** -0.5)
    kc, vc, gc = chunks(k), chunks(v), chunks(gk)
    b = jnp.cumsum(gc, axis=-2)
    b_mid = b[..., GLA_CHUNK // 2:GLA_CHUNK // 2 + 1, :]
    b_last = b[..., -1:, :]
    att = jnp.einsum('bhnid,bhnjd->bhnij', qc * jnp.exp(b - b_mid), kc * jnp.exp(b_mid - b))
    causal = jnp.tril(jnp.ones((GLA_CHUNK, GLA_CHUNK), dtype=bool))
    att = jnp.where(causal, att, 0.0)
    o_intra = jnp.einsum('bhnij,bhnjv->bhniv', att, vc)
    chunk_kv = jnp.einsum('bhnjd,bhnjv->nbhdv', kc * jnp.exp(b_last - b), vc)
    chunk_decay = jnp.exp(b_last[..., 0, :]).transpose(2, 0, 1, 3)
    def step(state, inp):
        kv, dec = inp
        return dec[..., None] * state + kv, state
    _, states = lax.scan(step, jnp.zeros((B, H, DK, DV), jnp.float32), (chunk_kv, chunk_decay))
    o_inter = jnp.einsum('bhnid,nbhdv->bhniv', qc * jnp.exp(b), states)
    o = (o_intra + o_inter).transpose(0, 2, 3, 1, 4).reshape(B, T, H, DV)
    return o.astype(v.dtype)

def hier_moe(xn, router_group, router_expert, w_gate, w_up, w_down):
    xf = xn.astype(jnp.float32)
    g_logits = xf @ router_group.astype(jnp.float32)
    g_prob = jax.nn.softmax(g_logits, axis=-1)
    g_idx = jnp.argmax(g_logits, axis=-1)
    g_w = jnp.take_along_axis(g_prob, g_idx[:, None], axis=-1)
    e_logits_all = jnp.einsum('nd,gde->nge', xf, router_expert.astype(jnp.float32))
    e_logits = jnp.take_along_axis(e_logits_all, g_idx[:, None, None], axis=1)[:, 0]
    top_v, top_i = lax.top_k(e_logits, EXPERT_TOP_K)
    top_p = jax.nn.softmax(top_v, axis=-1) * g_w
    e_w = jnp.sum(jax.nn.one_hot(top_i, EXPERTS_PER_GROUP, dtype=jnp.float32) * top_p[..., None], axis=1)
    combine = (jax.nn.one_hot(g_idx, N_GROUPS, dtype=jnp.float32)[:, :, None] * e_w[:, None, :]).astype(xn.dtype)
    y = jnp.zeros_like(xn)
    for g in range(N_GROUPS):
        hg = jax.nn.silu(jnp.einsum('nd,edf->nef', xn, w_gate[g])) * jnp.einsum('nd,edf->nef', xn, w_up[g])
        y = y + jnp.einsum('nef,efd->nd', hg * combine[:, g, :, None], w_down[g])
    return y

def hybrid_layer(h, valid, pos, norm1_w, w_in, q_norm_w, k_norm_w, attn_sinks, gla_gate_up,
                 gla_gate_bias, gla_norm_w, w_attn_branch, w_gla_branch, w_out, norm2_w,
                 router_group, router_expert, expert_w_gate, expert_w_up, expert_w_down):
    B, T, D = h.shape
    xn = rms_norm(h, norm1_w)
    proj = xn @ w_in
    parts = []
    off = 0
    for w in IN_WIDTHS:
        parts.append(proj[..., off:off + w])
        off += w
    qa, ka, va, qg, kg, vg, rg, gdown, gate_a, gate_g = parts
    qa = rope(rms_norm(qa.reshape(B, T, ATTN_HEADS, HEAD_DIM), q_norm_w), pos)
    ka = rope(rms_norm(ka.reshape(B, T, ATTN_KV_HEADS, HEAD_DIM), k_norm_w), pos)
    va = va.reshape(B, T, ATTN_KV_HEADS, HEAD_DIM)
    y_attn = swa_with_sinks(qa, ka, va, attn_sinks) @ w_attn_branch
    gk = jax.nn.log_sigmoid((gdown @ gla_gate_up + gla_gate_bias).astype(jnp.float32)) / GLA_GATE_NORM
    gk = gk.reshape(B, T, GLA_HEADS, GLA_KEY_DIM)
    kg = kg.reshape(B, T, GLA_HEADS, GLA_KEY_DIM) * valid[None, :, None, None]
    og = gla_chunked(qg.reshape(B, T, GLA_HEADS, GLA_KEY_DIM), kg,
                     vg.reshape(B, T, GLA_HEADS, GLA_VAL_DIM), gk)
    og = rms_norm(og, gla_norm_w) * jax.nn.silu(rg.reshape(B, T, GLA_HEADS, GLA_VAL_DIM))
    y_gla = og.reshape(B, T, GLA_V_W) @ w_gla_branch
    merged = jax.nn.sigmoid(gate_a) * y_attn + jax.nn.sigmoid(gate_g) * y_gla
    h = h + (merged @ w_out) * valid[None, :, None]
    xn2 = rms_norm(h, norm2_w).reshape(B * T, D)
    y_ffn = hier_moe(xn2, router_group, router_expert, expert_w_gate, expert_w_up, expert_w_down)
    return h + y_ffn.reshape(B, T, D) * valid[None, :, None]

def setup_inputs(seed: int = 0) -> dict:
    key = jax.random.key(seed)
    ks = jax.random.split(key, 20)
    f32 = jnp.float32
    def nrm(k, shape, scale):
        return jax.random.normal(k, shape, f32) * scale
    L = DEPTH
    E = EXPERTS_PER_GROUP
    return {
        "x": nrm(ks[0], (BATCH, SEQ, D_MODEL), 1.0),
        "meta_tokens": nrm(ks[1], (N_META, D_MODEL), 1.0),
        "norm1_w": 1.0 + nrm(ks[2], (L, D_MODEL), 0.02),
        "w_in": nrm(ks[3], (L, D_MODEL, IN_TOTAL), D_MODEL ** -0.5),
        "q_norm_w": 1.0 + nrm(ks[4], (L, HEAD_DIM), 0.02),
        "k_norm_w": 1.0 + nrm(ks[5], (L, HEAD_DIM), 0.02),
        "attn_sinks": nrm(ks[6], (L, ATTN_HEADS), 0.5),
        "gla_gate_up": nrm(ks[7], (L, GLA_GATE_RANK, GLA_K_W), GLA_GATE_RANK ** -0.5),
        "gla_gate_bias": nrm(ks[8], (L, GLA_K_W), 0.02),
        "gla_norm_w": 1.0 + nrm(ks[9], (L, GLA_VAL_DIM), 0.02),
        "w_attn_branch": nrm(ks[10], (L, ATTN_Q_W, D_MODEL), ATTN_Q_W ** -0.5),
        "w_gla_branch": nrm(ks[11], (L, GLA_V_W, D_MODEL), GLA_V_W ** -0.5),
        "w_out": nrm(ks[12], (L, D_MODEL, D_MODEL), D_MODEL ** -0.5),
        "norm2_w": 1.0 + nrm(ks[13], (L, D_MODEL), 0.02),
        "router_group": nrm(ks[14], (L, D_MODEL, N_GROUPS), D_MODEL ** -0.5),
        "router_expert": nrm(ks[15], (L, N_GROUPS, D_MODEL, E), D_MODEL ** -0.5),
        "expert_w_gate": nrm(ks[16], (L, N_GROUPS, E, D_MODEL, EXPERT_FF), D_MODEL ** -0.5),
        "expert_w_up": nrm(ks[17], (L, N_GROUPS, E, D_MODEL, EXPERT_FF), D_MODEL ** -0.5),
        "expert_w_down": nrm(ks[18], (L, N_GROUPS, E, EXPERT_FF, D_MODEL), EXPERT_FF ** -0.5),
    }

def reference(x, meta_tokens, norm1_w, w_in, q_norm_w, k_norm_w, attn_sinks, gla_gate_up,
              gla_gate_bias, gla_norm_w, w_attn_branch, w_gla_branch, w_out, norm2_w,
              router_group, router_expert, expert_w_gate, expert_w_up, expert_w_down):
    B, S, D = x.shape
    meta = jnp.broadcast_to(meta_tokens.astype(x.dtype)[None], (B, N_META, D))
    h = jnp.concatenate([jnp.zeros((B, PAD_FRONT, D), x.dtype), meta, x], axis=1)
    T = h.shape[1]
    idx = jnp.arange(T)
    valid = (idx >= PAD_FRONT).astype(x.dtype)
    pos = idx - PAD_FRONT
    for l in range(DEPTH):
        h = hybrid_layer(h, valid, pos, norm1_w[l], w_in[l], q_norm_w[l], k_norm_w[l],
                         attn_sinks[l], gla_gate_up[l], gla_gate_bias[l], gla_norm_w[l],
                         w_attn_branch[l], w_gla_branch[l], w_out[l], norm2_w[l],
                         router_group[l], router_expert[l], expert_w_gate[l],
                         expert_w_up[l], expert_w_down[l])
    return h[:, BLOCK:]


_drawn_inputs = setup_inputs


def setup_inputs(seed=0):
    import zlib

    import numpy as np

    out = dict(_drawn_inputs(seed))
    spreads = {}
    factors = {'q_norm_w': 8.0,
     'k_norm_w': 7.59,
     'attn_sinks': 8.0,
     'gla_gate_bias': 7.129,
     'gla_norm_w': 3.216,
     'norm2_w': 2.89}
    for name, (base, spread) in spreads.items():
        noise = np.random.default_rng([zlib.crc32(name.encode()), seed]).standard_normal(out[name].shape)
        drawn = base * np.exp(spread * noise) if base else spread * noise
        out[name] = __import__('jax').numpy.asarray(drawn.astype(out[name].dtype))
    for name, factor in factors.items():
        out[name] = (out[name] * factor).astype(out[name].dtype)
    return out
```

```python
from contextlib import ExitStack

import numpy as np
import concourse.bass as bass
from concourse import mybir

F32 = mybir.dt.float32
F32R = mybir.dt.float32r
U32 = mybir.dt.uint32
I32 = mybir.dt.int32
ALU = mybir.AluOpType
ACT = mybir.ActivationFunctionType
AX = mybir.AxisListType

D = 1024
T = 512
P = 128
NB = T // P
KT = D // P
NM = 16
XC = NM + T
HQ, HKV, DH = 8, 2, 64
GH, GK, GV = 4, 64, 128
GC = 64
NCH = T // GC
RANK = 16
NG, EPG, FF = 4, 8, 256
NE = NG * EPG
EPS = 1e-6
SCALE = DH ** -0.5
NEG = -1e30
CW = 256
SLOT = 64
PAIRS = NE // 2

QA, KA, QG, KG, VG, RG, GD, GA, GG = 0, 512, 768, 1024, 1280, 1792, 2304, 2320, 3344

CST = {}
_o = 0
for _n, _w in (("ident", 128), ("mask", 272), ("cc", NB * DH), ("ss", NB * DH), ("ccm", DH), ("ssm", DH),
               ("slots", SLOT), ("tri", 128), ("tok", NB), ("gi", NG), ("ei", EPG), ("eoff", NE)):
    CST[_n] = (_o, _o + _w)
    _o += _w
NCST = _o


def shape_tables():
    c = np.zeros((P, NCST), np.float32)

    def put(name, value):
        a, b = CST[name]
        c[:value.shape[0], a:b] = value.reshape(value.shape[0], -1)

    i, j = np.arange(P)[:, None], np.arange(P)[None, :]
    put("ident", np.eye(P, dtype=np.float32))
    prev = np.where(j > i, 0.0, NEG)
    own = np.where(j <= i, 0.0, NEG)
    put("mask", np.concatenate([prev, own, np.zeros((P, NM))], 1).astype(np.float32))
    half = DH // 2
    inv = np.float32(10000.0) ** (-(np.arange(half, dtype=np.float32) * np.float32(2.0)) / np.float32(DH))

    def angles(pos):
        a = pos.astype(np.float32)[..., None] * inv
        return (np.concatenate([np.cos(a), np.cos(a)], -1), np.concatenate([-np.sin(a), np.sin(a)], -1))

    cc, ss = angles(NM + np.arange(T).reshape(NB, P).T)
    put("cc", cc)
    put("ss", ss)
    cc, ss = angles(np.arange(NM))
    put("ccm", cc)
    put("ssm", ss)
    put("slots", np.tile(np.arange(SLOT, dtype=np.float32), (P, 1)))
    put("tri", (i < j).astype(np.float32))
    put("tok", (i + P * np.arange(NB)[None, :]).astype(np.float32))
    put("gi", np.tile(np.arange(NG, dtype=np.float32), (P, 1)))
    put("ei", np.tile(np.arange(EPG, dtype=np.float32), (P, 1)))
    put("eoff", np.tile(np.arange(NE, dtype=np.float32) * SLOT, (P, 1)))
    return c


class Banks:

    def __init__(self, tiles, full, free, families):
        self.tiles, self.full, self.free, self.families = tiles, full, free, families
        self.uses = [0] * len(tiles)
        self.turn = {f: 0 for f in families}
        self.where = {}

    def take(self, pe, family, name):
        ring = self.families[family]
        b = ring[self.turn[family] % len(ring)]
        self.turn[family] += 1
        if self.uses[b]:
            pe.wait_ge(self.free[b], self.uses[b])
        self.uses[b] += 1
        self.where[name] = (b, self.uses[b])
        return self.tiles[b]

    def done(self, name):
        return self.full[self.where[name][0]]

    def filled(self, name):
        b, n = self.where[name]
        return self.full[b], n

    def get(self, name):
        return self.tiles[self.where[name][0]]

    def read(self, name):
        return self.free[self.where[name][0]]

    def emptied(self, name):
        b, n = self.where[name]
        return self.free[b], n


def weight_chunks():
    out = [("gd", GD, RANK, KT), ("qg", QG, CW, KT), ("kg", KG, CW, KT), ("vg", VG, CW, KT), ("vg", VG + CW, CW, KT),
           ("kva", KA, CW, KT), ("qa", QA, CW, KT), ("qa", QA + CW, CW, KT), ("rg", RG, CW, KT), ("rg", RG + CW, CW, KT)]
    for q in range(4):
        out += [("ga", GA + q * CW, CW, KT), ("gg", GG + q * CW, CW, KT)]
    for half in range(2):
        out += [("wg", half * 512, 512, 4), ("wa", half * 512, 512, 4)]
    out += [("wo", q * CW, CW, KT) for q in range(4)]
    return out


CHUNKS = weight_chunks()
NCHUNK = len(CHUNKS)
CONST_DMAS = 18


def last_unit(c):
    kind = CHUNKS[c][0]
    if kind in ("gd", "kg", "vg", "kva"):
        return ("unit", c, "m")
    return ("unit", c, 1 if kind in ("qg", "ga", "gg") else 3)


def schedule():
    s = [("prep", 0), ("prep", 1), ("xT",)]
    s += [("unit", 0, 0), ("unit", 0, "m"), ("z",)]
    s += [("prep", 2), ("unit", 1, 0), ("unit", 1, 1)]
    s += [("prep", 3), ("unit", 2, 0), ("unit", 2, 1), ("unit", 2, "m")]
    s += [("prep", 4)] + [("unit", 3, 0), ("decay",)] + [("unit", 3, u) for u in (1, 2, 3, "m")]
    s += [("prep", 5)] + [("unit", 4, u) for u in (0, 1, 2, 3, "m")]
    s += [("prep", 6)] + [("unit", 5, u) for u in (0, 1, 2, 3, "m")] + [("krope",)]
    s += [("prep", 7), ("unit", 6, 0), ("kdm",), ("unit", 6, 1), ("kd", 0), ("kd", 1), ("kv", -1), ("unit", 6, 2),
          ("kd", 2), ("kd", 3), ("kv", 0), ("unit", 6, 3), ("kv", 1)]
    s += [("prep", 8)]
    for b in range(NB):
        s += [("unit", 7, b), ("qrope", b)]
        if b < 3:
            s += [("kv", 2 + b)]
    s += [("kv", 5), ("kv", 6)]
    s += [("prep", 9)]
    for b in range(NB):
        s += [("unit", 8, b), ("attT", b)] + ([("kT",)] if b == 0 else [])
        if b >= 1:
            s += [("glao", b - 1)]
    s += [("prep", 10)]
    for b in range(NB):
        s += [("unit", 9, b)] + ([("glao", NB - 1)] if b == 0 else []) + [("qT", b), ("ognorm", b)]
    n = 0
    late = []
    for c in range(10, 18):
        s += [("prep", c + 1)]
        for u in range(2):
            s += [("unit", c, u)]
            b, pair = divmod(n, 4)
            s += [("S", b, pair)] + late
            late = [("PV", b, pair)] + ([("onorm", b)] if pair == 3 else [])
            if pair == 2:
                s += [("ogT", b)]
            if pair == 1 and b >= 1:
                s += [("oT", b - 1)]
            n += 1
    s += [("prep", 19), ("unit", 18, 0)] + late + [("unit", 18, 1), ("unit", 18, 2), ("oT", NB - 1), ("unit", 18, 3)]
    for c in range(19, NCHUNK):
        s += [("prep", c + 1)] if c + 1 < NCHUNK else []
        s += [("unit", c, u) for u in range(4)]
    return s


SCHEDULE = schedule()


def layer_kernel(nc, x, meta_tokens, norm1_w, w_in, q_norm_w, k_norm_w, attn_sinks, gla_gate_up, gla_gate_bias,
                 gla_norm_w, w_attn_branch, w_gla_branch, w_out, norm2_w, router_group, router_expert,
                 expert_w_gate, expert_w_up, expert_w_down, table, xn_rows, y_rows, out):
    with ExitStack() as ctx:
        def sb(name, shape, dt=F32):
            return ctx.enter_context(nc.sbuf_tensor(name, shape, dt))

        def sem(name):
            return ctx.enter_context(nc.semaphore(name))

        h = sb("h", [P, NB, D])
        cst = sb("cst", [P, NCST])
        norm1 = sb("norm1", [P, KT])
        norm2 = sb("norm2", [P, KT])
        qk_w = sb("qk_w", [P, 4, DH])
        gla_w = sb("gla_w", [P, GV])
        sinks = sb("sinks", [P, HQ])
        nsinks = sb("nsinks", [P, HQ])
        gate_up = sb("gate_up", [RANK + 1, GH * GK])
        router = sb("router", [P, KT, NG + NE])
        minus_half = sb("minus_half", [P, 16])
        ones = sb("ones", [P, P])
        stat = sb("stat", [P, 16])
        rstd = sb("rstd", [P, 16])

        def C(name, rows=P):
            a, b = CST[name]
            return cst[0:rows, a:b]

        ident = C("ident")

        arena_start = (nc.sbuf_base + 31) // 32 * 32
        arena_size = (nc.sbuf_usable_end - arena_start) // 32 * 32

        def at(name, offset, shape, dt=F32):
            size = int(np.prod(shape[1:])) * 4
            assert offset + size <= arena_size, (name, offset, size, arena_size)
            return nc.alloc_sbuf_tensor_at(name, shape, dt, offset=arena_start + offset)

        K1 = 1024
        wraw = [at(f"wraw{i}", i * 8 * K1, [P, KT * CW]) for i in range(2)]
        whi = [at(f"whi{i}", (16 + 8 * i) * K1, [P, KT * CW], F32R) for i in range(2)]
        wlo = [at(f"wlo{i}", (32 + 8 * i) * K1, [P, KT * CW], F32R) for i in range(2)]
        xhi = at("xhi", 48 * K1, [P, KT, XC], F32R)
        xlo = at("xlo", 48 * K1 + 16896, [P, KT, XC], F32R)
        mhi = at("mhi", 48 * K1, [P, KT, T], F32R)
        mlo = at("mlo", 64 * K1, [P, KT, T], F32R)
        G = 82 * K1
        g_b = at("g_b", G, [P, 2, T])
        g_d = at("g_d", G + 4 * K1, [P, 2, T])
        att = [at(f"att{i}", G + 2 * i * K1, [P, GH, P]) for i in range(2)]
        og = [at(f"og{i}", G + (24 + 2 * i) * K1, [P, 512]) for i in range(NB)]
        g_q1 = at("g_q1", G + 8 * K1, [P, 2, T])
        g_k1 = at("g_k1", G + 12 * K1, [P, 2, T])
        g_q3 = at("g_q3", G + 16 * K1, [P, 2, T])
        g_k4 = at("g_k4", G + 20 * K1, [P, 2, T])
        g_q = at("g_q", G + 24 * K1, [P, 2, T])
        g_k = at("g_k", G + 28 * K1, [P, 2, T])
        sig_a = at("sig_a", G, [P, KT, T])
        sig_g = at("sig_g", G + 16 * K1, [P, KT, T])
        vg = at("vg", G + 32 * K1, [P, NB, 512])
        kd = at("kd", G + 40 * K1, [P, NB, 256])
        st = at("st", G + 44 * K1, [P, NCH, 2, GV])
        ohi = at("ohi", G + 32 * K1, [P, 4, T], F32R)
        olo = at("olo", G + 40 * K1, [P, 4, T], F32R)
        rgs = at("rgs", G + 52 * K1, [P, NB, 512])
        tab = at("tab", G + 60 * K1, [P, 4, NB, DH])
        prob = [at(f"prob{i}", G + 60 * K1 + 1088 * i, [P, 272]) for i in range(4)]
        Q = G + 64 * K1 + 256
        qT = at("qT", Q, [P, 4, T])
        xm = at("xm", Q, [NM, D])
        xmf = at("xmf", Q + 4 * K1, [P, KT, NM])
        Y = Q + 8 * K1
        xr = at("xr", Y, [P, NB, D])
        q_tok = at("q_tok", Y, [P, NB, 512])
        n_sq = at("n_sq", Y + 8 * K1, [P, 512])
        n_x = at("n_x", Y + 10 * K1, [P, 512])
        n_t = at("n_t", Y + 12 * K1, [P, 512])
        vgm = at("vgm", Y + 14 * K1, [NM, 512])
        oghi = at("oghi", Y, [P, 4, T], F32R)
        oglo = at("oglo", Y + 8 * K1, [P, 4, T], F32R)
        ptm = [at(f"ptm{i}", 81 * K1 + 512 * i, [NM, P]) for i in range(2)]
        place = [Y + 16 * K1]

        def more(name, shape, dt=F32):
            t = at(name, place[0], shape, dt)
            place[0] += (int(np.prod(shape[1:])) * 4 + 31) // 32 * 32
            return t

        v_tok = more("v_tok", [P, NB, P])
        pt = [at(f"pt{i}", place[0] + K1 * i, [P, 256]) for i in range(2)]
        k_tok = more("k_tok", [P, NB, P])
        o_tok = at("o_tok", place[0], [P, 512])
        km = more("km", [NM, CW])
        kdm = more("kdm", [NM, CW])
        krm = more("krm", [NM, P])
        vm = more("vm", [NM, P])
        kT = more("kT", [P, XC])
        zm = more("zm", [P, 2, NM])
        lm = more("lm", [P, 2, NM])
        bm = more("bm", [P, 2, NM])
        kgm = more("kgm", [P, 2, NM])
        dec = more("dec", [P, 2 * NCH])
        tabm = more("tabm", [NM, 2, DH])
        att_stat = more("att_stat", [P, 2, 5, HQ])
        gdT = at("gdT", G + 64 * K1 + 256 + 4 * K1 + 512, [RANK + 1, XC])
        g_l = g_q1
        xj = at("xj", G + 32 * K1, [NM, D])
        reset = at("reset", Y + 16 * K1, [P, T])

        xs = at("xs", 0, [P, NB, D])
        xnT = at("xnT", 16 * K1, [P, KT, T])
        slot_of = at("slot_of", 32 * K1, [P, NB, NE * SLOT])
        place = [64 * K1]
        logits = more("logits", [P, NB, NG + NE])
        g4 = [more(f"g4_{i}", [P, NB, NG]) for i in range(3)]
        e8 = [more(f"e8_{i}", [P, NB, EPG]) for i in range(6)]
        b4 = [more(f"b4_{i}", [P, NB]) for i in range(12)]
        first_e = more("first_e", [P, NB, NE])
        second_e = more("second_e", [P, NB, NE])
        chosen = more("chosen", [P, NB, NE])
        token_w = more("token_w", [P, NB, 1 + NE])
        rank = more("rank", [P, NB, NE])
        r_tmp = more("r_tmp", [P, NB, NE])
        r_sel = more("r_sel", [P, NB, NE])
        counts = more("counts", [P, NE])
        pick_rank = more("pick_rank", [P, 2, NB])
        pick_base = more("pick_base", [P, 2, NB])
        pick_in = more("pick_in", [P, 2, NB])
        pick_low = more("pick_low", [P, 2, NB])
        row_of = more("row_of", [P, 2, NB], U32)
        n_round = more("n_round", [P, 4])
        rounds_i = more("rounds_i", [P, 1], I32)
        slot_tok = more("slot_tok", [P, PAIRS], U32)
        slot_w = more("slot_w", [P, PAIRS])
        waited = more("waited", [P, 4], U32)
        gather_i = [more(f"gather_i{i}", [P, 1], U32) for i in range(2)]
        pair_w = [more(f"pair_w{i}", [P, 1]) for i in range(2)]
        assert place[0] <= 82 * K1
        xg = [at(f"xg{i}", 4 * i * K1, [P, D]) for i in range(2)]
        xgT = at("xgT", 8 * K1, [P, KT, P])
        y = [at(f"y{i}", (16 + 4 * i) * K1, [P, D]) for i in range(2)]
        hs = [at(f"hs{i}", 24 * K1 + 512 * i, [P, 2, SLOT]) for i in range(2)]
        hg = [at(f"hg{i}", 25 * K1 + 512 * i, [P, 2, SLOT]) for i in range(2)]
        we = [[[at(f"w{n}{s}{j}", 82 * K1 + (3 * (2 * s + j) + i) * 8 * K1, shape)
                for i, (n, shape) in enumerate((("gate", [P, KT, FF]), ("up", [P, KT, FF]), ("down", [P, 2, D])))]
               for j in range(2)] for s in range(2)]
        picked = [at(f"picked{i}", (32 + 4 * i) * K1, [P, D]) for i in range(8)]

        def view(t, rows, groups):
            return t[0:rows, 0:groups * DH].rearrange("p (g d) -> p g d", d=DH)

        tiles = [ctx.enter_context(nc.psum_tensor(f"bank{i}", [P, 512], F32)) for i in range(8)]
        banks = Banks(tiles, [sem(f"bank{i}_full") for i in range(8)], [sem(f"bank{i}_free") for i in range(8)],
                      {"unit": [0, 1, 2], "S": [3, 4], "T": [5, 6], "O": [7]})

        s_x = [sem(f"x{b}_loaded") for b in range(NB)]
        s_meta = sem("meta_loaded")
        s_const = sem("constants_loaded")
        s_w = [sem(f"weights{i}_loaded") for i in range(2)]
        s_hi = sem("weights_hi")
        s_lo = sem("weights_lo")
        s_ones = sem("ones_set")
        s_out = sem("out_stored")
        s_set = sem("constants_set")
        s_set2 = sem("gate_rows_set")
        s_reset = sem("chunk_starts_set")
        s_sumsq = sem("x_squares_summed")
        s_mean = sem("x_means")
        s_rstd = sem("x_rstd")
        s_xr = sem("x_scaled")
        s_xhi = sem("xT_hi")
        s_xlo = sem("meta_xT_lo")
        s_z = sem("gate_logits_split")
        s_l = sem("log_terms")
        s_diff = sem("decay_differences")
        s_exp = sem("decay_exps")
        s_gla_in = sem("gla_inputs")
        s_square = sem("norm_squares")
        s_mean2 = sem("norm_means")
        s_krope = sem("k_roped")
        s_qrope = sem("q_roped")
        s_zero = sem("att_zeroed")
        s_attm = sem("att_masked")
        s_re = sem("rg_exp")
        s_rsilu = sem("rg_silu")
        s_ogn = sem("gla_out_normed")
        s_max = sem("score_max")
        s_prob = sem("probs_ready")
        s_es = sem("sink_terms")
        s_pv = sem("pv_done")
        s_ohi = sem("oT_hi")
        s_oghi = sem("ogT_hi")
        s_sig = sem("gates_ready")
        s_mer = sem("merged")
        s_mhi = sem("merged_hi")
        s_mlo = sem("merged_lo")
        s_h = sem("residual_ready")
        s_pe = sem("tensor_chain")
        s_dve = sem("vector_chain")
        s_act = sem("scalar_chain")
        s_pool = sem("gpsimd_chain")

        s_xs_loc = sem("rows_scaled")
        s_sq2 = sem("residual_squares")
        s_m2 = sem("residual_means")
        s_r2 = sem("residual_rstd")
        s_xs = sem("rows_stored")
        s_rank = sem("ranks_moved")
        s_rexp = sem("router_exps")
        s_rdiff = sem("router_differences")
        s_choice = sem("experts_chosen")
        s_rows = sem("rows_known")
        s_rounds = sem("rounds_known")
        s_slot_of = sem("slot_maps")
        s_slot_ps = sem("slots_multiplied")
        s_slots = sem("slots_known")
        s_gath = [sem(f"gathered{i}") for i in range(2)]
        s_gidx = sem("gather_index")
        s_T = sem("rows_transposed")
        s_xgT = sem("rows_ready")
        s_gu = [sem(f"gate_up{j}_done") for j in range(2)]
        s_silu = [sem(f"silu{j}_done") for j in range(2)]
        s_hg = [sem(f"hidden{j}_ready") for j in range(2)]
        s_down = sem("down_done")
        s_yv = sem("y_half_vector")
        s_ya = sem("y_half_scalar")
        s_pw = sem("pair_weight")
        s_yst = [sem(f"y{i}_stored") for i in range(2)]
        s_we = [[sem(f"expert_weights{s}{j}") for j in range(2)] for s in range(2)]
        s_pick = [sem(f"picked{i}") for i in range(8)]
        s_fin = sem("output_ready")

        def w_source(c):
            kind, c0, n, kt = CHUNKS[c]
            if kind == "wa":
                return w_attn_branch[0, :, c0:c0 + n].rearrange("(k p) n -> p k n", p=P)
            if kind == "wg":
                return w_gla_branch[0, :, c0:c0 + n].rearrange("(k p) n -> p k n", p=P)
            if kind == "wo":
                return w_out[0, :, c0:c0 + n].rearrange("(k p) n -> p k n", p=P)
            return w_in[0, :, c0:c0 + n].rearrange("(p k) n -> p k n", k=KT)

        def w_view(t, c):
            kind, c0, n, kt = CHUNKS[c]
            return t[:, 0:kt * n].rearrange("p (k n) -> p k n", k=kt)

        def q_heads(b, g):
            return q_tok[:, b, :].rearrange("p (i g d) -> p g i d", g=2, d=DH)[:, g, :, :]

        def head_before(n, k):
            m = n - k
            return (m // 8, m % 8 // 2, m % 2)

        def chain(eng, s):
            count = [0]

            def link(ins):
                count[0] += 1
                ins.then_inc(s, 1)
                eng.wait_ge(s, count[0])
            return link

        def chunks_of(t):
            return t[:, :, :].rearrange("p j (c t) -> p (j c) t", t=GC)

        block = ctx.enter_context(nc.Block())

        @block.tensor
        def _(pe):
            def mm3(ps, lhi, llo, rhi, rlo, kt):
                for k in range(kt):
                    nc.tensor.matmul(ps, lhi(k), rhi(k), start=(k == 0), stop=False)
                    nc.tensor.matmul(ps, lhi(k), rlo(k), start=False, stop=False)
                    last = nc.tensor.matmul(ps, llo(k), rhi(k), start=False, stop=(k == kt - 1))
                return last

            link = chain(pe, s_pe)

            def cols(t, a, b):
                return lambda k: t[:, k, a:b]

            pe.wait_ge(s_const, CONST_DMAS * 16)
            pe.wait_ge(s_ones, 1)
            for step in SCHEDULE:
                kind = step[0]
                if kind == "xT":
                    pe.wait_ge(s_xr, NB + 1)
                    for k in range(KT):
                        ps = banks.take(pe, "unit", ("xT", k))
                        for b in range(NB):
                            src = xr[:, b, :].rearrange("p (c k) -> p k c", k=KT)[:, k, :]
                            last = nc.tensor.transpose(ps[:, b * P:(b + 1) * P], src, ident)
                        last.then_inc(banks.done(("xT", k)), 1)
                    ps = banks.take(pe, "T", "xmT")
                    for k in range(KT):
                        src = xm[:, :].rearrange("p (c k) -> p k c", k=KT)[:, k, :]
                        last = nc.tensor.transpose(ps[:, k * NM:(k + 1) * NM], src, ident[0:NM, 0:NM])
                    last.then_inc(banks.done("xmT"), 1)
                elif kind == "unit":
                    _, c, u = step
                    name, c0, n, kt = CHUNKS[c]
                    if u == 0:
                        pe.wait_ge(s_lo, c + 1)
                    if c == 0 and u == 0:
                        for k in range(KT - 3, KT):
                            pe.wait_ge(*banks.emptied(("xT", k)))
                        pe.wait_ge(s_xlo, 1)
                    wh, wl = w_view(whi[c % 2], c), w_view(wlo[c % 2], c)
                    meta = u == "m"
                    xa, xb = (0, NM) if meta else (NM, XC)
                    if name in ("qg", "kg", "gd", "ga", "gg"):
                        if meta and name == "kg":
                            ps = banks.take(pe, "unit", step)
                            for j in range(2):
                                last = mm3(ps[:, j * NM:(j + 1) * NM], cols(wh, j * P, (j + 1) * P),
                                           cols(wl, j * P, (j + 1) * P), cols(xhi, xa, xb), cols(xlo, xa, xb), KT)
                        else:
                            ps = banks.take(pe, "unit", step)
                            a, b = (0, RANK) if name == "gd" else (u * P, (u + 1) * P)
                            last = mm3(ps[0:b - a, 0:xb - xa], cols(wh, a, b), cols(wl, a, b),
                                       cols(xhi, xa, xb), cols(xlo, xa, xb), KT)
                    elif name in ("vg", "kva", "qa", "rg"):
                        ps = banks.take(pe, "unit", step)
                        a, b = (0, NM) if meta else (NM + u * P, NM + (u + 1) * P)
                        last = mm3(ps[0:b - a, 0:n], cols(xhi, a, b), cols(xlo, a, b), cols(wh, 0, n), cols(wl, 0, n), KT)
                    elif name in ("wa", "wg"):
                        if u == 0 and c0 == 0:
                            for b in range(NB):
                                pe.wait_ge(*banks.emptied(("ogT" if name == "wg" else "oT", b)))
                        ih, il = (oghi, oglo) if name == "wg" else (ohi, olo)
                        ps = banks.take(pe, "unit", step)
                        last = mm3(ps[:, :], cols(wh, u * P, (u + 1) * P), cols(wl, u * P, (u + 1) * P),
                                   cols(ih, 0, T), cols(il, 0, T), 4)
                    else:
                        if c0 == 0 and u == 0:
                            pe.wait_ge(s_mlo, KT)
                        ps = banks.take(pe, "unit", step)
                        last = mm3(ps[:, 0:n], cols(mhi, u * P, (u + 1) * P), cols(mlo, u * P, (u + 1) * P),
                                   cols(wh, 0, n), cols(wl, 0, n), KT)
                    last.then_inc(banks.done(step), 1)
                elif kind == "z":
                    pe.wait_ge(*banks.emptied(("unit", 0, 0)))
                    pe.wait_ge(*banks.emptied(("unit", 0, "m")))
                    for j in range(2):
                        ps = banks.take(pe, "unit", ("z", j))
                        nc.tensor.matmul(ps[:, :], gate_up[:, j * P:(j + 1) * P], gdT[:, NM:XC],
                                         start=True, stop=True).then_inc(banks.done(("z", j)), 1)
                    ps = banks.take(pe, "T", "zm")
                    for j in range(2):
                        last = nc.tensor.matmul(ps[:, j * NM:(j + 1) * NM], gate_up[:, j * P:(j + 1) * P],
                                                gdT[:, 0:NM], start=True, stop=True)
                    last.then_inc(banks.done("zm"), 1)
                elif kind == "kdm":
                    pe.wait_ge(s_gla_in, 5)
                    ps = banks.take(pe, "T", "kdm")
                    for j in range(2):
                        last = nc.tensor.transpose(ps[0:NM, j * P:(j + 1) * P], kgm[:, j, :], ident)
                    last.then_inc(banks.done("kdm"), 1)
                elif kind == "kd":
                    b = step[1]
                    ps = banks.take(pe, "T", step)
                    for j in range(2):
                        last = nc.tensor.transpose(ps[:, j * P:(j + 1) * P], g_k4[:, j, b * P:(b + 1) * P], ident)
                    last.then_inc(banks.done(step), 1)
                elif kind == "kv":
                    c = step[1]
                    ps = banks.take(pe, "S", step)
                    if c < 0:
                        pe.wait_ge(*banks.emptied("kdm"))
                        pe.wait_ge(*banks.emptied(("unit", 3, "m")))
                        pe.wait_ge(*banks.emptied(("unit", 4, "m")))
                    else:
                        pe.wait_ge(*banks.emptied(("kd", c // 2)))
                    for hd in range(GH):
                        a = (hd % 2) * GK
                        o = ps[a:a + GK, (hd // 2) * GV:(hd // 2 + 1) * GV]
                        if c < 0:
                            lhs, rhs = kdm[:, hd * GK:(hd + 1) * GK], vgm[:, hd * GV:(hd + 1) * GV]
                        else:
                            t0 = (c % 2) * GC
                            lhs = kd[t0:t0 + GC, c // 2, hd * GK:(hd + 1) * GK]
                            rhs = vg[t0:t0 + GC, c // 2, hd * GV:(hd + 1) * GV]
                        last = nc.tensor.matmul(o, lhs, rhs, start=True, stop=True)
                    last.then_inc(banks.done(step), 1)
                elif kind == "attT":
                    b = step[1]
                    ps = banks.take(pe, "S", step)
                    for hd in (0, 2, 1, 3):
                        a = (hd % 2) * GK
                        last = nc.tensor.matmul(ps[:, hd * P:(hd + 1) * P],
                                                g_k1[a:a + GK, hd // 2, b * P:(b + 1) * P],
                                                g_q1[a:a + GK, hd // 2, b * P:(b + 1) * P], start=True, stop=True)
                        if hd == 2:
                            link(last)
                    last.then_inc(banks.done(step), 1)
                elif kind == "glao":
                    b = step[1]
                    ps = banks.take(pe, "O", step)
                    pe.wait_ge(s_attm, b + 1)
                    pe.wait_ge(*banks.emptied(("kv", 2 * b)))
                    for hd in (0, 2, 1, 3):
                        a = (hd % 2) * GK
                        o = ps[:, hd * GV:(hd + 1) * GV]
                        nc.tensor.matmul(o, att[b % 2][:, hd, :], vg[:, b, hd * GV:(hd + 1) * GV],
                                         start=True, stop=False)
                        for s in range(2):
                            t0 = b * P + s * GC
                            last = nc.tensor.matmul(ps[s * GC:(s + 1) * GC, hd * GV:(hd + 1) * GV],
                                                    g_q3[a:a + GK, hd // 2, t0:t0 + GC],
                                                    st[a:a + GK, 2 * b + s, hd // 2, :],
                                                    start=False, stop=True)
                        if hd == 2:
                            link(last)
                    last.then_inc(banks.done(step), 1)
                elif kind == "kT":
                    pe.wait_ge(s_krope, 2)
                    ps = banks.take(pe, "T", "kT")
                    for b in range(NB):
                        last = nc.tensor.transpose(ps[:, b * P:(b + 1) * P], k_tok[:, b, :], ident)
                    last.then_inc(banks.done("kT"), 1)
                    ps = banks.take(pe, "T", "kTm")
                    nc.tensor.transpose(ps[:, 0:NM], krm[:, :], ident[0:NM, 0:NM]).then_inc(banks.done("kTm"), 1)
                elif kind == "qT":
                    b = step[1]
                    pe.wait_ge(s_qrope, b + 1)
                    ps = banks.take(pe, "T", step)
                    for i in range(4):
                        last = nc.tensor.transpose(ps[:, i * P:(i + 1) * P], q_tok[:, b, i * P:(i + 1) * P], ident)
                    last.then_inc(banks.done(step), 1)
                elif kind == "S":
                    _, b, i = step
                    if i == 0:
                        pe.wait_ge(*banks.emptied(("qT", b)))
                    if i == 0 and b == 0:
                        pe.wait_ge(*banks.emptied("kT"))
                        pe.wait_ge(*banks.emptied("kTm"))
                    for j in range(2):
                        ps = banks.take(pe, "S", ("S", b, i, j))
                        q = qT[j * DH:(j + 1) * DH, i, b * P:(b + 1) * P]
                        if b == 0:
                            nc.tensor.matmul(ps[:, 128:256], q, kT[j * DH:(j + 1) * DH, NM:NM + P], start=True, stop=True)
                        else:
                            nc.tensor.matmul(ps[:, 0:256], q, kT[j * DH:(j + 1) * DH, NM + (b - 1) * P:NM + (b + 1) * P],
                                             start=True, stop=True)
                        nc.tensor.matmul(ps[:, 256:272], q, kT[j * DH:(j + 1) * DH, 0:NM],
                                         start=True, stop=True).then_inc(banks.done(("S", b, i, j)), 1)
                elif kind == "PV":
                    _, b, i = step
                    n0 = 2 * (4 * b + i)
                    for j in range(2):
                        pe.wait_ge(s_prob, n0 + j + 1)
                        ps = banks.take(pe, "T", ("PT", b, i, j))
                        p = prob[(n0 + j) % 4]
                        if b > 0:
                            nc.tensor.transpose(ps[:, 0:128], p[:, 0:128], ident)
                        nc.tensor.transpose(ps[:, 128:256], p[:, 128:256], ident)
                        nc.tensor.transpose(ps[0:NM, 256:384], p[:, 256:272], ident).then_inc(banks.done(("PT", b, i, j)), 1)
                    if i == 0:
                        pv = banks.take(pe, "O", ("PV", b))
                    for j in range(2):
                        pe.wait_ge(*banks.emptied(("PT", b, i, j)))
                        hd = j * 4 + i
                        o = pv[:, hd * DH:(hd + 1) * DH]
                        vc = slice(j * DH, (j + 1) * DH)
                        if b > 0:
                            nc.tensor.matmul(o, pt[j][:, 0:128], v_tok[:, b - 1, vc], start=True, stop=False)
                        nc.tensor.matmul(o, pt[j][:, 128:256], v_tok[:, b, vc], start=(b == 0), stop=False)
                        last = nc.tensor.matmul(o, ptm[j][:, :], vm[:, vc],
                                                start=False, stop=True)
                    last.then_inc(s_pv, 1)
                elif kind in ("oT", "ogT"):
                    b = step[1]
                    if kind == "oT":
                        pe.wait_ge(*banks.emptied(("PV", b)))
                    else:
                        pe.wait_ge(s_ogn, b + 1)
                    src = o_tok[:, :] if kind == "oT" else rgs[:, b, :]
                    ps = banks.take(pe, "T", step)
                    for j in range(4):
                        last = nc.tensor.transpose(ps[:, j * P:(j + 1) * P], src[:, j * P:(j + 1) * P], ident)
                    last.then_inc(banks.done(step), 1)

            for b in range(NB):
                pe.wait_ge(s_xs_loc, b + 1)
                for half in range(2):
                    ps = banks.take(pe, "unit", ("nT", b, half))
                    for k in range(4):
                        src = xs[:, b, :].rearrange("p (c k) -> p k c", k=KT)[:, 4 * half + k, :]
                        last = nc.tensor.transpose(ps[:, k * P:(k + 1) * P], src, ident)
                    last.then_inc(banks.done(("nT", b, half)), 1)
                ps = banks.take(pe, "S", ("logit", b))
                for half in range(2):
                    pe.wait_ge(*banks.emptied(("nT", b, half)))
                    for k in range(4 * half, 4 * half + 4):
                        last = nc.tensor.matmul(ps[:, 0:NG + NE], xnT[:, k, b * P:(b + 1) * P], router[:, k, :],
                                                start=(k == 0), stop=(k == KT - 1))
                last.then_inc(banks.done(("logit", b)), 1)
            pe.wait_ge(s_choice, 1)
            ps = banks.take(pe, "S", "rank")
            for b in range(NB + 1):
                for b2 in range(min(b + 1, NB)):
                    last = nc.tensor.matmul(ps[:, b * NE:(b + 1) * NE], C("tri") if b2 == b else ones[:, :],
                                            chosen[:, b2, :], start=(b2 == 0), stop=(b2 == min(b, NB - 1)))
            last.then_inc(banks.done("rank"), 1)

            pe.wait_ge(*banks.emptied("rank"))
            pe.wait_ge(s_rounds, 1)
            rounds = pe.value_load(rounds_i[0:1, 0:1], min_val=1, max_val=T // SLOT)
            with pe.Fori(0, rounds) as r:
                pe.wait_ge(s_slot_of, (r + 1) * NB)
                for m in range(PAIRS):
                    for b in range(NB):
                        last = nc.tensor.matmul(tiles[5 + m // 8][:, m % 8 * 33:(m % 8 + 1) * 33],
                                                slot_of[:, b, m * P:(m + 1) * P], token_w[:, b, :],
                                                start=(b == 0), stop=(b == NB - 1))
                last.then_inc(s_slot_ps, 1)
                with pe.Fori(0, PAIRS // 2) as i:
                    q = r * (PAIRS // 2) + i
                    for s in range(2):
                        pe.wait_ge(s_gath[s], 16 * q + 16)
                        for k in range(KT):
                            src = xg[s][:, :].rearrange("p (c k) -> p k c", k=KT)[:, k, :]
                            last = nc.tensor.transpose(tiles[5 + k // 4][:, k % 4 * P:(k % 4 + 1) * P], src, ident)
                        last.then_inc(s_T, 1)
                        pe.wait_ge(s_xgT, 2 * q + s + 1)
                        for j in range(2):
                            pe.wait_ge(s_we[s][j], 48 * q + 48)
                            for f in range(4):
                                w = we[s][j][f // 2]
                                for k in range(KT):
                                    last = nc.tensor.matmul(tiles[3 + j][:, f * SLOT:(f + 1) * SLOT],
                                                            w[:, k, f % 2 * P:(f % 2 + 1) * P],
                                                            xgT[:, k, j * SLOT:(j + 1) * SLOT],
                                                            start=(k == 0), stop=(k == KT - 1))
                            last.then_inc(s_gu[j], 1)
                        pe.wait_ge(s_yv, 2 * q + s + 1)
                        pe.wait_ge(s_ya, 2 * q + s + 1)
                        for j in range(2):
                            pe.wait_ge(s_hg[j], 2 * q + s + 1)
                            for half in range(2):
                                for f in range(2):
                                    last = nc.tensor.matmul(tiles[half][j * SLOT:(j + 1) * SLOT, :], hg[j][:, f, :],
                                                            we[s][j][2][:, f, half * 512:(half + 1) * 512],
                                                            start=(f == 0), stop=(f == 1))
                        last.then_inc(s_down, 1)

        @block.sync
        def _(sp):
            def load_w(c):
                if c >= 2:
                    sp.wait_ge(s_lo, c - 1)
                sp.dma_start(w_view(wraw[c % 2], c), w_source(c)).then_inc(s_w[c % 2], 16)

            for started in (s_T, s_yv, s_ya, s_fin, s_yst[0], s_yst[1]):
                sp.sem_inc(started, 1)
            for b in range(NB):
                sp.dma_start(h[:, b, :], x[0, b * P:(b + 1) * P, :]).then_inc(s_x[b], 16)
            sp.dma_start(xm[:, :], meta_tokens).then_inc(s_meta, 16)
            for c in range(NCHUNK):
                load_w(c)
            def load_pair(pair, s):
                for j in range(2):
                    e = pair * 2 + j
                    for i, w in enumerate((expert_w_gate, expert_w_up, expert_w_down)):
                        src = w[0].rearrange("g e a n -> (g e) a n")[bass.ds(e, 1), :, :]
                        src = src.rearrange("o (p k) n -> p (o k) n", p=P) if i < 2 else \
                            src.rearrange("o (k p) n -> p (o k) n", p=P)
                        sp.dma_start(we[s][j][i][:, :, :], src).then_inc(s_we[s][j], 16)

            sp.wait_ge(s_mlo, KT)
            for s in range(2):
                load_pair(s, s)
            for b in range(NB):
                sp.wait_ge(s_xs_loc, b + 1)
                sp.dma_start(xn_rows[b * P:(b + 1) * P, :], xs[:, b, :]).then_inc(s_xs, 16)
            with sp.Fori(1, PAIRS // 2) as i:
                for s in range(2):
                    sp.wait_ge(s_down, 2 * i + s - 1)
                    load_pair(2 * i + s, s)
            sp.wait_ge(s_rounds, 1)
            rounds = sp.value_load(rounds_i[0:1, 0:1], min_val=1, max_val=T // SLOT)
            with sp.If(rounds > 1):
                with sp.Fori(1, rounds) as r:
                    with sp.Fori(0, PAIRS // 2) as i:
                        for s in range(2):
                            sp.wait_ge(s_down, r * PAIRS + 2 * i + s - 1)
                            load_pair(2 * i + s, s)
            sp.wait_ge(s_fin, rounds * (2 * NB) + 1)
            for b in range(NB):
                sp.dma_start(out[0, b * P:(b + 1) * P, :], h[:, b, :]).then_inc(s_out, 16)
            sp.wait_ge(s_out, 16 * NB)

        @block.scalar
        def _(act):
            link = chain(act, s_act)
            q0, k0 = q_norm_w[0, :], k_norm_w[0, :]
            hh = DH // 2
            consts = [(cst[:, :], table), (norm1[:, :], norm1_w[0].rearrange("(p k) -> p k", k=KT)),
                      (norm2[:, :], norm2_w[0].rearrange("(p k) -> p k", k=KT)),
                      (qk_w[:, 0, :], q0.partition_broadcast(P)),
                      (qk_w[:, 1, 0:hh], q0[hh:DH].partition_broadcast(P)),
                      (qk_w[:, 1, hh:DH], q0[0:hh].partition_broadcast(P)),
                      (qk_w[:, 2, :], k0.partition_broadcast(P)),
                      (qk_w[:, 3, 0:hh], k0[hh:DH].partition_broadcast(P)),
                      (qk_w[:, 3, hh:DH], k0[0:hh].partition_broadcast(P)),
                      (gla_w[:, :], gla_norm_w[0, :].partition_broadcast(P)),
                      (sinks[:, :], attn_sinks[0, :].partition_broadcast(P)),
                      (gate_up[0:RANK, :], gla_gate_up[0]), (gate_up[RANK:RANK + 1, :], gla_gate_bias),
                      (router[:, :, 0:NG], router_group[0].rearrange("(p k) g -> p k g", k=KT))]
            consts += [(router[:, :, NG + EPG * g:NG + EPG * (g + 1)],
                        router_expert[0, g].rearrange("(p k) e -> p k e", k=KT)) for g in range(NG)]
            assert len(consts) == CONST_DMAS
            for dst, src in consts:
                act.dma_start(dst, src).then_inc(s_const, 16)

            for step in SCHEDULE:
                kind = step[0]
                if kind == "prep":
                    c = step[1]
                    act.wait_ge(s_w[c % 2], 16 * (c // 2 + 1))
                    if c >= 2:
                        act.wait_ge(*banks.filled(last_unit(c - 2)))
                    nc.scalar.activation(w_view(whi[c % 2], c), w_view(wraw[c % 2], c), ACT.Copy).then_inc(s_hi, 1)
                elif kind == "xT":
                    act.wait_ge(s_set, 2)
                    for b in range(NB):
                        act.wait_ge(s_x[b], 16)
                        nc.scalar.activation(xr[:, b, :], h[:, b, :], ACT.Square,
                                             accum_out=stat[:, b:b + 1]).then_inc(s_sumsq, 1)
                    act.wait_ge(s_meta, 16)
                    nc.scalar.activation(xj[:, :], xm[:, :], ACT.Square,
                                         accum_out=stat[0:NM, NB:NB + 1]).then_inc(s_sumsq, 1)
                    act.wait_ge(s_const, CONST_DMAS * 16)
                    for k in range(KT):
                        act.wait_ge(*banks.filled(("xT", k)))
                        nc.scalar.activation(xhi[:, k, NM:XC], banks.get(("xT", k))[:, :], ACT.Copy,
                                             scale=norm1[:, k:k + 1]).then_inc(s_xhi, 1)
                    act.wait_ge(*banks.emptied("xmT"))
                    nc.scalar.activation(xhi[:, :, 0:NM], xmf[:, :, :], ACT.Copy).then_inc(s_xhi, 1)
                elif kind == "unit":
                    _, c, u = step
                    name, c0, n, kt = CHUNKS[c]
                    if name == "wa":
                        j = c0 // P + u
                        act.wait_ge(s_mer, j + 1)
                        nc.scalar.activation(mhi[:, j, :], sig_a[:, j, :], ACT.Copy).then_inc(s_mhi, 1)
                        continue
                    if name == "vg" and c == 4 or name == "qa" and c == 7 or name in ("wg", "wo"):
                        continue
                    if name in ("ga", "gg") and (c, u) == (10, 0):
                        act.wait_ge(*banks.filled(("glao", NB - 1)))
                        act.wait_ge(s_ogn, NB)
                    act.wait_ge(*banks.filled(step))
                    ps = banks.get(step)
                    if name == "gd":
                        act.wait_ge(s_set2, 1)
                        dst, src = (gdT[0:RANK, NM:XC], ps[0:RANK, :]) if u == 0 else (gdT[0:RANK, 0:NM], ps[0:RANK, 0:NM])
                        nc.scalar.activation(dst, src, ACT.Copy).then_inc(banks.read(step), 1)
                    elif name == "qg":
                        nc.scalar.activation(g_q[:, u, :], ps[:, :], ACT.Copy, scale=GK ** -0.5).then_inc(banks.read(step), 1)
                    elif name == "kg" and u != "m":
                        nc.scalar.activation(g_k[:, u, :], ps[:, :], ACT.Copy).then_inc(banks.read(step), 1)
                    elif name == "kg":
                        nc.scalar.activation(kgm[:, :, :], ps[:, 0:2 * NM], ACT.Copy).then_inc(banks.read(step), 1)
                    elif name == "vg":
                        dst = vgm[:, 0:CW] if u == "m" else vg[:, u, 0:CW]
                        nc.scalar.activation(dst, ps[0:NM if u == "m" else P, 0:CW], ACT.Copy).then_inc(banks.read(step), 1)
                    elif name == "kva":
                        kd_, vd_, r = (km[:, 0:P], vm[:, :], NM) if u == "m" else (k_tok[:, u, :], v_tok[:, u, :], P)
                        nc.scalar.activation(kd_, ps[0:r, 0:P], ACT.Copy)
                        nc.scalar.activation(vd_, ps[0:r, P:2 * P], ACT.Copy).then_inc(banks.read(step), 1)
                    elif name == "qa":
                        nc.scalar.activation(q_heads(u, 0), ps[:, 0:CW].rearrange("p (i d) -> p i d", d=DH), ACT.Copy).then_inc(banks.read(step), 1)
                    elif name == "rg":
                        o = (c - 8) * CW
                        nc.scalar.activation(rgs[:, u, o:o + CW], ps[:, 0:CW], ACT.Exp, scale=-1.0).then_inc(s_re, 1)
                    else:
                        j = (c - 10) // 2 * 2 + u
                        dst = sig_a if name == "ga" else sig_g
                        nc.scalar.activation(dst[:, j, :], ps[:, :], ACT.Exp, scale=-1.0).then_inc(banks.read(step), 1)
                elif kind == "z":
                    for j in range(3):
                        act.wait_ge(*banks.emptied(("z", j) if j < 2 else "zm"))
                        dst, src = (g_l[:, j, :], g_d[:, j, :]) if j < 2 else (lm[:, :, :], zm[:, :, :])
                        link(nc.scalar.activation(dst, src, ACT.Exp, scale=-1.0))
                    for j in range(3):
                        dst = g_l[:, j, :] if j < 2 else lm[:, :, :]
                        nc.scalar.activation(dst, dst, ACT.Ln, bias=1.0).then_inc(s_l, 1)
                elif kind == "decay":
                    s = 1.0 / 16.0
                    act.wait_ge(s_diff, 1)
                    nc.scalar.activation(g_q1[:, :, :], g_d[:, :, :], ACT.Exp, scale=s).then_inc(s_exp, 1)
                    nc.scalar.activation(g_k1[:, :, :], g_d[:, :, :], ACT.Exp, scale=-s).then_inc(s_exp, 1)
                    nc.scalar.activation(g_q3[:, :, :], g_b[:, :, :], ACT.Exp, scale=s).then_inc(s_exp, 1)
                    act.wait_ge(s_diff, 2)
                    nc.scalar.activation(g_k4[:, :, :], g_k4[:, :, :], ACT.Exp, scale=s).then_inc(s_exp, 1)
                    act.wait_ge(s_diff, 3)
                    nc.scalar.activation(lm[:, :, :], lm[:, :, :], ACT.Exp, scale=s).then_inc(s_exp, 1)
                    nc.scalar.activation(dec[:, :], chunks_of(g_b)[:, :, GC - 1], ACT.Exp, scale=s).then_inc(s_exp, 1)
                elif kind == "attT":
                    b = step[1]
                    act.wait_ge(*banks.filled(step))
                    act.wait_ge(s_zero, 2)
                    if b >= 2:
                        act.wait_ge(*banks.filled(("glao", b - 2)))
                    ps = banks.get(step)[:, :].rearrange("p (h i) -> p h i", h=GH)
                    nc.scalar.activation(att[b % 2][0:GC, :, 0:GC], ps[0:GC, :, 0:GC], ACT.Copy)
                    nc.scalar.activation(att[b % 2][GC:P, :, GC:P], ps[GC:P, :, GC:P], ACT.Copy).then_inc(banks.read(step), 1)
                elif kind == "glao":
                    b = step[1]
                    act.wait_ge(*banks.filled(step))
                    nc.scalar.activation(og[b][:, :], banks.get(step)[:, :], ACT.Copy).then_inc(banks.read(step), 1)
                elif kind == "kT":
                    act.wait_ge(*banks.filled("kT"))
                    nc.scalar.activation(kT[:, NM:XC], banks.get("kT")[:, :], ACT.Copy).then_inc(banks.read("kT"), 1)
                    act.wait_ge(*banks.filled("kTm"))
                    nc.scalar.activation(kT[:, 0:NM], banks.get("kTm")[:, 0:NM], ACT.Copy).then_inc(banks.read("kTm"), 1)
                elif kind == "qT":
                    b = step[1]
                    act.wait_ge(*banks.filled(step))
                    ps = banks.get(step)[:, :].rearrange("p (i t) -> p i t", i=4)
                    nc.scalar.activation(qT[:, :, b * P:(b + 1) * P], ps, ACT.Copy).then_inc(banks.read(step), 1)
                elif kind == "S":
                    _, b, i = step
                    for j in range(2):
                        n = 2 * (4 * b + i) + j
                        hd = j * 4 + i
                        act.wait_ge(s_max, n + 1)
                        st_ = att_stat[:, b % 2, :, hd:hd + 1]
                        p = prob[n % 4][:, 128 if b == 0 else 0:272]
                        nc.scalar.activation(p, p, ACT.Exp, bias=st_[:, 1, :], scale=SCALE,
                                             accum_out=st_[:, 2, :]).then_inc(s_prob, 1)
                        nc.scalar.activation(st_[:, 3, :], sinks[:, hd:hd + 1], ACT.Exp,
                                             bias=st_[:, 1, :]).then_inc(s_es, 1)
                elif kind == "PV":
                    _, b, i = step
                    name = ("PT", b, i, 0)
                    act.wait_ge(*banks.filled(name))
                    if 4 * b + i:
                        act.wait_ge(s_pv, 4 * b + i)
                    ps = banks.get(name)
                    c0 = 128 if b == 0 else 0
                    nc.scalar.activation(pt[0][:, c0:256], ps[:, c0:256], ACT.Copy)
                    nc.scalar.activation(ptm[0][:, :], ps[0:NM, 256:384], ACT.Copy).then_inc(banks.read(name), 1)
                elif kind in ("oT", "ogT"):
                    b = step[1]
                    act.wait_ge(*banks.filled(step))
                    dst, s = (ohi, s_ohi) if kind == "oT" else (oghi, s_oghi)
                    ps = banks.get(step)[:, :].rearrange("p (j t) -> p j t", j=4)
                    nc.scalar.activation(dst[:, :, b * P:(b + 1) * P], ps, ACT.Copy).then_inc(s, 1)

            for b in range(NB):
                for c in range(22, 26):
                    act.wait_ge(*banks.emptied(("unit", c, b)))
                nc.scalar.activation(xs[:, b, :], h[:, b, :], ACT.Square, accum_out=stat[:, b:b + 1]).then_inc(s_sq2, 1)
            act.wait_ge(s_rdiff, 1)
            nc.scalar.activation(g4[0][:, :, :], g4[0][:, :, :], ACT.Exp).then_inc(s_rexp, 1)
            act.wait_ge(s_rdiff, 2)
            nc.scalar.activation(b4[4][:, :], b4[4][:, :], ACT.Exp).then_inc(s_rexp, 1)

            act.wait_ge(s_rounds, 1)
            rounds = act.value_load(rounds_i[0:1, 0:1], min_val=1, max_val=T // SLOT)
            y_store = y_rows.rearrange("(e t) d -> e t d", e=NE)
            with act.Fori(0, rounds) as r:
                act.wait_ge(s_fin, r * (2 * NB) + 1)
                with act.Fori(0, PAIRS // 2) as i:
                    q = r * (PAIRS // 2) + i
                    for s in range(2):
                        for j in range(2):
                            act.wait_ge(s_gu[j], 2 * q + s + 1)
                            nc.scalar.activation(hs[j][:, :, :], tiles[3 + j][:, 0:2 * SLOT].rearrange("p (f t) -> p f t", f=2),
                                                 ACT.Silu).then_inc(s_silu[j], 1)
                        act.wait_ge(s_down, 2 * q + s + 1)
                        act.wait_ge(s_pw, 2 * q + s + 1)
                        act.wait_ge(s_yst[s], 32 * q + 1)
                        nc.scalar.activation(y[s][:, 512:D], tiles[1][:, :], ACT.Copy,
                                             scale=pair_w[s][:, 0:1]).then_inc(s_ya, 1)
                        act.wait_ge(s_ya, 2 * q + s + 2)
                        act.wait_ge(s_yv, 2 * q + s + 2)
                        for j in range(2):
                            dst = y_store[bass.ds(4 * i + 2 * s + j, 1), bass.ds(0, SLOT), :]
                            act.dma_start(dst.rearrange("o t d -> (o t) d"), y[s][j * SLOT:(j + 1) * SLOT, :]).then_inc(s_yst[s], 16)

        @block.vector
        def _(dve):
            link = chain(dve, s_dve)
            norms = [0]

            def norm_mean(src, rows, groups, width):
                norms[0] += 1
                dve.wait_ge(s_square, norms[0])
                link(nc.vector.tensor_reduce(stat[0:rows, 0:groups], src, AX.X, ALU.add))
                nc.vector.tensor_scalar(stat[0:rows, 0:groups], stat[0:rows, 0:groups], 1.0 / width, EPS,
                                        ALU.mult, ALU.add).then_inc(s_mean2, 1)

            nc.vector.memset(stat[:, :], 1.0).then_inc(s_set, 1)
            nc.vector.memset(ones[:, :], 1.0).then_inc(s_ones, 1)
            nc.vector.memset(minus_half[:, :], -0.5).then_inc(s_set, 1)
            for step in SCHEDULE:
                kind = step[0]
                if kind == "prep":
                    c = step[1]
                    dve.wait_ge(s_hi, c + 1)
                    nc.vector.tensor_tensor(w_view(wlo[c % 2], c), w_view(wraw[c % 2], c),
                                            w_view(whi[c % 2], c).bitcast(F32), ALU.subtract).then_inc(s_lo, 1)
                elif kind == "xT":
                    dve.wait_ge(s_sumsq, NB + 1)
                    nc.vector.tensor_scalar(stat[:, 0:NB + 1], stat[:, 0:NB + 1], 1.0 / D, EPS,
                                            ALU.mult, ALU.add).then_inc(s_mean, 1)
                    dve.wait_ge(s_rstd, 1)
                    for b in range(NB):
                        nc.vector.tensor_scalar(xr[:, b, :], h[:, b, :], rstd[:, b:b + 1], None, ALU.mult).then_inc(s_xr, 1)
                    nc.vector.tensor_scalar(xm[:, :], xm[:, :], rstd[0:NM, NB:NB + 1], None, ALU.mult).then_inc(s_xr, 1)
                    dve.wait_ge(s_const, CONST_DMAS * 16)
                    nc.vector.tensor_scalar(nsinks[:, :], sinks[:, :], -1.0, None, ALU.mult).then_inc(s_set, 1)
                    for k in range(KT):
                        dve.wait_ge(s_xhi, k + 1)
                        nc.vector.scalar_tensor_tensor(xlo[:, k, NM:XC], banks.get(("xT", k))[:, :], norm1[:, k:k + 1],
                                                       xhi[:, k, NM:XC].bitcast(F32), ALU.mult, ALU.subtract)\
                            .then_inc(banks.read(("xT", k)), 1)
                    dve.wait_ge(*banks.filled("xmT"))
                    ps = banks.get("xmT")[:, 0:KT * NM].rearrange("p (k m) -> p k m", k=KT)
                    nc.vector.tensor_tensor(xmf[:, :, :], ps, norm1[:, :].unsqueeze(2).to_broadcast([P, KT, NM]),
                                            ALU.mult).then_inc(banks.read("xmT"), 1)
                    dve.wait_ge(s_xhi, KT + 1)
                    nc.vector.tensor_tensor(xlo[:, :, 0:NM], xmf[:, :, :], xhi[:, :, 0:NM].bitcast(F32),
                                            ALU.subtract).then_inc(s_xlo, 1)
                elif kind == "unit":
                    _, c, u = step
                    name, c0, n, kt = CHUNKS[c]
                    if name == "vg" and c == 4:
                        dve.wait_ge(*banks.filled(step))
                        dst = vgm[:, CW:2 * CW] if u == "m" else vg[:, u, CW:2 * CW]
                        nc.vector.tensor_copy(dst, banks.get(step)[0:NM if u == "m" else P, 0:CW]).then_inc(banks.read(step), 1)
                    elif name == "qa" and c == 7:
                        dve.wait_ge(*banks.filled(step))
                        nc.vector.tensor_copy(q_heads(u, 1), banks.get(step)[:, 0:CW].rearrange("p (i d) -> p i d", d=DH)).then_inc(banks.read(step), 1)
                    elif name == "rg":
                        dve.wait_ge(s_re, (c - 8) * NB + u + 1)
                        r = rgs[:, u, (c - 8) * CW:(c - 7) * CW]
                        link(nc.vector.tensor_scalar(r, r, 1.0, None, ALU.add))
                        link(nc.vector.reciprocal(r, r))
                        nc.vector.tensor_tensor(r, banks.get(step)[:, 0:CW], r, ALU.mult).then_inc(banks.read(step), 1)
                    elif name in ("ga", "gg"):
                        j = (c - 10) // 2 * 2 + u
                        t = (sig_a if name == "ga" else sig_g)[:, j, :]
                        dve.wait_ge(*banks.emptied(step))
                        link(nc.vector.tensor_scalar(t, t, 1.0, None, ALU.add))
                        nc.vector.reciprocal(t, t).then_inc(s_sig, 1)
                    elif name in ("wa", "wg"):
                        j = c0 // P + u
                        t = (sig_a if name == "wa" else sig_g)[:, j, :]
                        dve.wait_ge(s_sig, 16)
                        dve.wait_ge(*banks.filled(step))
                        nc.vector.tensor_tensor(t, banks.get(step)[:, :], t, ALU.mult).then_inc(banks.read(step), 1)
                        if name == "wa":
                            dve.wait_ge(*banks.emptied(step))
                            dve.wait_ge(*banks.emptied(("unit", c - 1, u)))
                            nc.vector.tensor_tensor(t, t, sig_g[:, j, :], ALU.add).then_inc(s_mer, 1)
                            dve.wait_ge(s_mhi, j + 1)
                            nc.vector.tensor_tensor(mlo[:, j, :], t, mhi[:, j, :].bitcast(F32), ALU.subtract).then_inc(s_mlo, 1)
                    elif name == "wo":
                        dve.wait_ge(*banks.filled(step))
                        nc.vector.tensor_tensor(h[:, u, c0:c0 + n], banks.get(step)[:, 0:n], h[:, u, c0:c0 + n],
                                                ALU.add).then_inc(banks.read(step), 1)
                elif kind == "z":
                    for j in range(2):
                        dve.wait_ge(*banks.filled(("z", j)))
                        ps = banks.get(("z", j))
                        link(nc.vector.tensor_single_scalar(g_q3[:, j, :], ps[:, :], 0.0, ALU.min))
                        nc.vector.scalar_tensor_tensor(g_d[:, j, :], g_q3[:, j, :], -2.0, ps[:, :], ALU.mult, ALU.add)\
                            .then_inc(banks.read(("z", j)), 1)
                    dve.wait_ge(*banks.filled("zm"))
                    ps = banks.get("zm")[:, 0:2 * NM]
                    zf, bf = (t[:, :, :].rearrange("p j m -> p (j m)") for t in (zm, bm))
                    link(nc.vector.tensor_single_scalar(bf, ps, 0.0, ALU.min))
                    nc.vector.scalar_tensor_tensor(zf, bf, -2.0, ps, ALU.mult, ALU.add).then_inc(banks.read("zm"), 1)
                    for j in range(2):
                        dve.wait_ge(s_l, j + 1)
                        dve.wait_ge(*banks.emptied(("z", j)))
                        link(nc.vector.tensor_tensor(g_q3[:, j, :], g_q3[:, j, :], g_l[:, j, :], ALU.subtract))
                        dve.wait_ge(s_reset, 2)
                        link(nc.vector.tensor_tensor_scan(g_b[:, j, :], reset[:, :], g_q3[:, j, :], 0.0, ALU.mult, ALU.add))
                    dve.wait_ge(s_l, 3)
                    dve.wait_ge(*banks.emptied("zm"))
                    link(nc.vector.tensor_tensor(bm[:, :, :], bm[:, :, :], lm[:, :, :], ALU.subtract))
                    for j in range(2):
                        link(nc.vector.tensor_tensor_scan(zm[:, j, :], ones[:, 0:NM], bm[:, j, :], 0.0, ALU.mult, ALU.add))
                    bv, dv, k4 = chunks_of(g_b), chunks_of(g_d), chunks_of(g_k4)
                    full = [P, 2 * NCH, GC]
                    nc.vector.tensor_tensor(dv, bv, bv[:, :, GC // 2:GC // 2 + 1].to_broadcast(full), ALU.subtract).then_inc(s_diff, 1)
                    nc.vector.tensor_tensor(k4, bv[:, :, GC - 1:GC].to_broadcast(full), bv, ALU.subtract).then_inc(s_diff, 1)
                    nc.vector.tensor_tensor(lm[:, :, :], zm[:, :, NM - 1:NM].to_broadcast([P, 2, NM]), zm[:, :, :],
                                            ALU.subtract).then_inc(s_diff, 1)
                elif kind == "decay":
                    for j in range(2):
                        dve.wait_ge(*banks.emptied(("unit", 1, j)))
                        dve.wait_ge(*banks.emptied(("unit", 2, j)))
                    dve.wait_ge(*banks.emptied(("unit", 2, "m")))
                    for i, (t, o) in enumerate(((g_q1, g_q), (g_k1, g_k), (g_q3, g_q), (g_k4, g_k), (kgm, lm))):
                        dve.wait_ge(s_exp, i + 1)
                        nc.vector.tensor_tensor(t[:, :, :], t[:, :, :], o[:, :, :], ALU.mult).then_inc(s_gla_in, 1)
                elif kind == "kdm":
                    dve.wait_ge(*banks.filled("kdm"))
                    nc.vector.tensor_copy(kdm[:, :], banks.get("kdm")[0:NM, 0:CW]).then_inc(banks.read("kdm"), 1)
                elif kind == "kd":
                    dve.wait_ge(*banks.filled(step))
                    nc.vector.tensor_copy(kd[:, step[1], :], banks.get(step)[:, 0:CW]).then_inc(banks.read(step), 1)
                elif kind == "kv":
                    c = step[1]
                    dve.wait_ge(*banks.filled(step))
                    ps = banks.get(step)
                    if c < 0:
                        nc.vector.tensor_copy(st[:, 0, :, :], ps[:, 0:2 * GV].rearrange("p (j v) -> p j v", j=2))\
                            .then_inc(banks.read(step), 1)
                    else:
                        dve.wait_ge(s_exp, 6)
                        dve.wait_ge(*banks.emptied(("kv", c - 1)))
                        for j in range(2):
                            last = nc.vector.scalar_tensor_tensor(st[:, c + 1, j, :], st[:, c, j, :],
                                                                  dec[:, j * NCH + c:j * NCH + c + 1],
                                                                  ps[:, j * GV:(j + 1) * GV], ALU.mult, ALU.add)
                        last.then_inc(banks.read(step), 1)
                elif kind == "krope":
                    norm_mean(n_sq[:, :].rearrange("p (g d) -> p g d", d=DH), P, 8, DH)
                    norm_mean(n_sq[0:NM, 0:P].rearrange("p (g d) -> p g d", d=DH), NM, HKV, DH)
                elif kind == "qrope":
                    norm_mean(n_sq[:, :].rearrange("p (g d) -> p g d", d=DH), P, HQ, DH)
                elif kind == "ognorm":
                    norm_mean(n_sq[:, :].rearrange("p (g d) -> p g d", d=GV), P, GH, GV)
                elif kind == "S":
                    _, b, i = step
                    if (b, i) == (0, 0):
                        dve.wait_ge(s_qrope, NB)
                    for j in range(2):
                        n = 2 * (4 * b + i) + j
                        hd = j * 4 + i
                        name = ("S", b, i, j)
                        st_ = att_stat[:, b % 2, :, hd:hd + 1]
                        c0 = 128 if b == 0 else 0
                        dve.wait_ge(*banks.filled(name))
                        if n >= 4:
                            dve.wait_ge(*banks.filled(("PT",) + head_before(n, 4)))
                        nc.vector.tensor_tensor_reduce(out=prob[n % 4][:, c0:272], in0=banks.get(name)[:, c0:272],
                                                       in1=C("mask")[:, c0:272], scale=1.0, scalar=-3.0e38,
                                                       op0=ALU.add, op1=ALU.max, accum_out=st_[:, 0, :])\
                            .then_inc(banks.read(name), 1)
                        dve.wait_ge(*banks.emptied(name))
                        nc.vector.tensor_scalar(st_[:, 1, :], st_[:, 0, :], -SCALE, nsinks[:, hd:hd + 1],
                                                ALU.mult, ALU.min).then_inc(s_max, 1)
                elif kind == "PV":
                    _, b, i = step
                    name = ("PT", b, i, 1)
                    dve.wait_ge(*banks.filled(name))
                    if 4 * b + i:
                        dve.wait_ge(s_pv, 4 * b + i)
                    ps = banks.get(name)
                    c0 = 128 if b == 0 else 0
                    nc.vector.tensor_copy(pt[1][:, c0:256], ps[:, c0:256])
                    nc.vector.tensor_copy(ptm[1][:, :], ps[0:NM, 256:384]).then_inc(banks.read(name), 1)
                elif kind == "onorm":
                    b = step[1]
                    st_ = att_stat[:, b % 2, :, :]
                    dve.wait_ge(s_es, 8 * (b + 1))
                    link(nc.vector.tensor_tensor(st_[:, 4, :], st_[:, 2, :], st_[:, 3, :], ALU.add))
                    link(nc.vector.reciprocal(st_[:, 4, :], st_[:, 4, :]))
                    dve.wait_ge(s_pv, 4 * (b + 1))
                    if b:
                        dve.wait_ge(*banks.filled(("oT", b - 1)))
                    nc.vector.tensor_tensor(o_tok[:, :].rearrange("p (h d) -> p h d", d=DH),
                                            banks.get(("PV", b))[:, :].rearrange("p (h d) -> p h d", d=DH),
                                            st_[:, 4, :].unsqueeze(2).to_broadcast([P, HQ, DH]), ALU.mult)\
                        .then_inc(banks.read(("PV", b)), 1)
                elif kind in ("oT", "ogT"):
                    b = step[1]
                    dst, hi, s = (olo, ohi, s_ohi) if kind == "oT" else (oglo, oghi, s_oghi)
                    dve.wait_ge(s, b + 1)
                    if kind == "ogT" and b == 0:
                        dve.wait_ge(s_ogn, NB)
                    cb = slice(b * P, (b + 1) * P)
                    nc.vector.tensor_tensor(dst[:, :, cb], banks.get(step)[:, :].rearrange("p (j t) -> p j t", j=4),
                                            hi[:, :, cb].bitcast(F32), ALU.subtract).then_inc(banks.read(step), 1)

            def tt(o, a, b, op):
                return link(nc.vector.tensor_tensor(o, a, b, op))

            dve.wait_ge(s_sq2, NB)
            nc.vector.tensor_scalar(stat[:, 0:NB], stat[:, 0:NB], 1.0 / D, EPS, ALU.mult, ALU.add).then_inc(s_m2, 1)
            dve.wait_ge(s_r2, 1)
            for b in range(NB):
                nc.vector.tensor_scalar(xs[:, b, :], h[:, b, :], rstd[:, b:b + 1], None, ALU.mult).then_inc(s_xs_loc, 1)
            for b in range(NB):
                for half in range(2):
                    name = ("nT", b, half)
                    dve.wait_ge(*banks.filled(name))
                    nc.vector.tensor_tensor(xnT[:, 4 * half:4 * half + 4, b * P:(b + 1) * P],
                                            banks.get(name)[:, :].rearrange("p (k t) -> p k t", k=4),
                                            norm2[:, 4 * half:4 * half + 4].unsqueeze(2).to_broadcast([P, 4, P]),
                                            ALU.mult).then_inc(banks.read(name), 1)
                dve.wait_ge(*banks.filled(("logit", b)))
                nc.vector.tensor_copy(logits[:, b, :], banks.get(("logit", b))[:, 0:NG + NE]).then_inc(banks.read(("logit", b)), 1)
            for b in (2, 3):
                dve.wait_ge(*banks.emptied(("logit", b)))

            def bc(t, shape, axis=2):
                return t.unsqueeze(axis).to_broadcast(shape)

            def first_max(v, onehot, maxv, tmp, idx, numbers, n):
                full = [P, NB, n]
                link(nc.vector.tensor_reduce(maxv, v, AX.X, ALU.max))
                tt(tmp, v, bc(maxv, full), ALU.is_lt)
                link(nc.vector.scalar_tensor_tensor(tmp, tmp, 1000.0, bc(numbers, full, 1), ALU.mult, ALU.add))
                link(nc.vector.tensor_reduce(idx, tmp, AX.X, ALU.min))
                tt(onehot, bc(numbers, full, 1), bc(idx, full), ALU.is_equal)

            gl = logits[:, :, 0:NG]
            group, g_tmp = g4[1][:, :, :], g4[2][:, :, :]
            gmax, gw, v1, v2, p2, p1, idx, rec = (b4[i][:, :] for i in (0, 1, 2, 3, 4, 5, 6, 7))
            first_max(gl, group, gmax, g_tmp, idx, C("gi"), NG)
            nc.vector.tensor_tensor(g4[0][:, :, :], gl, bc(gmax, [P, NB, NG]), ALU.subtract).then_inc(s_rdiff, 1)
            el = logits[:, :, NG:NG + NE].rearrange("p b (g e) -> p b g e", g=NG)
            four = [P, NB, NG, EPG]
            sel = r_tmp[:, :, :].rearrange("p b (g e) -> p b g e", g=NG)
            tt(sel, el, bc(group, four, 3), ALU.mult)
            ev, ev2, one1, one2, e_tmp = (t[:, :, :] for t in e8[0:5])
            link(nc.vector.tensor_reduce(ev, sel.rearrange("p b g e -> p b e g"), AX.X, ALU.add))
            first_max(ev, one1, v1, e_tmp, idx, C("ei"), EPG)
            link(nc.vector.scalar_tensor_tensor(ev2, one1, -3.0e38, ev, ALU.mult, ALU.add))
            first_max(ev2, one2, v2, e_tmp, idx, C("ei"), EPG)
            nc.vector.tensor_tensor(b4[4][:, :], v2, v1, ALU.subtract).then_inc(s_rdiff, 1)
            for onehot, dst in ((one1, first_e), (one2, second_e)):
                tt(dst[:, :, :].rearrange("p b (g e) -> p b g e", g=NG), bc(onehot, four, 2), bc(group, four, 3), ALU.mult)
            nc.vector.tensor_tensor(chosen[:, :, :], first_e[:, :, :], second_e[:, :, :], ALU.add).then_inc(s_choice, 1)
            dve.wait_ge(s_rexp, 2)
            link(nc.vector.tensor_reduce(gw, g4[0][:, :, :], AX.X, ALU.add))
            link(nc.vector.tensor_scalar(rec, p2, 1.0, None, ALU.add))
            tt(rec, rec, gw, ALU.mult)
            link(nc.vector.reciprocal(p1, rec))
            tt(p2, p2, p1, ALU.mult)
            all_e = [P, NB, NE]
            tt(r_tmp[:, :, :], first_e[:, :, :], bc(p1, all_e), ALU.mult)
            tt(r_sel[:, :, :], second_e[:, :, :], bc(p2, all_e), ALU.mult)
            tt(token_w[:, :, 1:1 + NE], r_tmp[:, :, :], r_sel[:, :, :], ALU.add)
            link(nc.vector.tensor_copy(token_w[:, :, 0], C("tok")))
            dve.wait_ge(*banks.filled("rank"))
            ps = banks.get("rank")
            link(nc.vector.tensor_copy(rank[:, :, :].rearrange("p b e -> p (b e)"), ps[:, 0:NB * NE]))
            nc.vector.tensor_copy(counts[:, :], ps[:, NB * NE:(NB + 1) * NE]).then_inc(banks.read("rank"), 1)
            dve.wait_ge(*banks.emptied("rank"))
            link(nc.vector.tensor_reduce(n_round[:, 0:1], counts[:, :], AX.X, ALU.max))
            link(nc.vector.tensor_scalar(e8[5][:, 0, :], C("slots")[:, 0:T // SLOT], float(SLOT), n_round[:, 0:1],
                                         ALU.mult, ALU.is_lt))
            link(nc.vector.tensor_reduce(n_round[:, 1:2], e8[5][:, 0, :], AX.X, ALU.add))
            nc.vector.tensor_copy(rounds_i[:, :], n_round[:, 1:2]).then_inc(s_rounds, 1)
            for i, onehot in enumerate((first_e, second_e)):
                for dst, what in ((pick_rank, rank[:, :, :]), (pick_base, bc(C("eoff"), all_e, 1))):
                    tt(r_sel[:, :, :], what, onehot[:, :, :], ALU.mult)
                    link(nc.vector.tensor_reduce(dst[:, i, :], r_sel[:, :, :], AX.X, ALU.add))
            link(nc.vector.scalar_tensor_tensor(rank[:, :, :], rank[:, :, :], 1.0, chosen[:, :, :], ALU.add, ALU.mult))
            link(nc.vector.tensor_scalar(rank[:, :, :], rank[:, :, :], -1.0, None, ALU.add))

            dve.wait_ge(s_rounds, 1)
            dve.wait_ge(s_xs, 16 * NB)
            rounds = dve.value_load(rounds_i[0:1, 0:1], min_val=1, max_val=T // SLOT)
            with dve.Fori(0, rounds) as r:
                def step_of(ins, k):
                    ins.then_inc(s_rank, 1)
                    dve.wait_ge(s_rank, 5 * r + k + 1)

                for b in range(NB):
                    full = [P, NE, SLOT]
                    nc.vector.tensor_tensor(slot_of[:, b, :].rearrange("p (e s) -> p e s", e=NE), bc(C("slots"), full, 1),
                                            bc(rank[:, b, :], full), ALU.is_equal).then_inc(s_slot_of, 1)
                dve.wait_ge(s_slot_of, (r + 1) * NB)
                step_of(nc.vector.tensor_scalar(pick_low[:, :, :], pick_rank[:, :, :], 0.0, None, ALU.is_ge), 0)
                step_of(nc.vector.scalar_tensor_tensor(pick_in[:, :, :], pick_rank[:, :, :], float(SLOT),
                                                       pick_low[:, :, :], ALU.is_lt, ALU.mult), 1)
                step_of(nc.vector.tensor_tensor(pick_low[:, :, :], pick_rank[:, :, :], pick_in[:, :, :], ALU.mult), 2)
                nc.vector.tensor_tensor(row_of[:, :, :], pick_low[:, :, :], pick_base[:, :, :], ALU.add).then_inc(s_rows, 1)
                nc.vector.tensor_scalar(pick_rank[:, :, :], pick_rank[:, :, :], -float(SLOT), None, ALU.add).then_inc(s_rank, 1)
                nc.vector.tensor_scalar(rank[:, :, :], rank[:, :, :], -float(SLOT), None, ALU.add).then_inc(s_rank, 1)
                dve.wait_ge(s_rank, 5 * r + 5)
                dve.wait_ge(s_slot_ps, r + 1)
                for g in range(2):
                    ps = tiles[5 + g]
                    nc.vector.tensor_copy(slot_tok[:, 8 * g:8 * g + 8], ps[:, 0:8 * 33:33])
                    for j in range(2):
                        c0 = 1 + 16 * g + j
                        last = nc.vector.tensor_copy(slot_w[j * SLOT:(j + 1) * SLOT, 8 * g:8 * g + 8],
                                                     ps[j * SLOT:(j + 1) * SLOT, c0:c0 + 7 * 35 + 1:35])
                last.then_inc(s_slots, 1)
                with dve.Fori(0, PAIRS // 2) as i:
                    q = r * (PAIRS // 2) + i
                    for s in range(2):
                        dve.wait_ge(s_T, 2 * q + s + 2)
                        for g in range(2):
                            last = nc.vector.tensor_tensor(xgT[:, 4 * g:4 * g + 4, :],
                                                           tiles[5 + g][:, :].rearrange("p (k t) -> p k t", k=4),
                                                           bc(norm2[:, 4 * g:4 * g + 4], [P, 4, P]), ALU.mult)
                        last.then_inc(s_xgT, 1)
                        dve.wait_ge(s_slots, r + 1)
                        nc.vector.tensor_copy(pair_w[s][:, :], slot_w[:, bass.ds(2 * i + s, 1)]).then_inc(s_pw, 1)
                        for j in range(2):
                            dve.wait_ge(s_silu[j], 2 * q + s + 1)
                            nc.vector.tensor_tensor(hg[j][:, :, :], hs[j][:, :, :],
                                                    tiles[3 + j][:, 2 * SLOT:4 * SLOT].rearrange("p (f t) -> p f t", f=2),
                                                    ALU.mult).then_inc(s_hg[j], 1)
                        dve.wait_ge(s_down, 2 * q + s + 1)
                        dve.wait_ge(s_pw, 2 * q + s + 1)
                        dve.wait_ge(s_yst[s], 32 * q + 1)
                        nc.vector.tensor_scalar(y[s][:, 0:512], tiles[0][:, :], pair_w[s][:, 0:1], None,
                                                ALU.mult).then_inc(s_yv, 1)

                for b in range(NB):
                    for i in range(2):
                        dve.wait_ge(s_pick[2 * b + i], 16 * r + 16)
                        nc.vector.scalar_tensor_tensor(h[:, b, :], picked[2 * b + i][:, :], pick_in[:, i, b:b + 1],
                                                       h[:, b, :], ALU.mult, ALU.add).then_inc(s_fin, 1)
                        dve.wait_ge(s_fin, r * (2 * NB) + 2 * b + i + 2)

        @block.gpsimd
        def _(pool):
            link = chain(pool, s_pool)
            norms = [0]

            def tt(o, a, b, op=ALU.mult):
                return nc.gpsimd.tensor_tensor(o, a, b, op)

            def rms(src, sq, rows, groups):
                norms[0] += 1
                tt(sq, src, src).then_inc(s_square, 1)
                pool.wait_ge(s_mean2, norms[0])
                link(tt(rstd[0:rows, 0:groups], stat[0:rows, 0:groups], minus_half[0:rows, 0:groups], ALU.pow))

            def rope(x_, cosw, sinw, xn, t, dst, rows, groups, done, count):
                hh = DH // 2
                rms(x_, t, rows, groups)
                link(tt(xn, x_, rstd[0:rows, 0:groups].unsqueeze(2).to_broadcast([rows, groups, DH])))
                tt(t[:, :, 0:hh], xn[:, :, hh:DH], sinw[:, :, 0:hh])
                link(tt(t[:, :, hh:DH], xn[:, :, 0:hh], sinw[:, :, hh:DH]))
                link(tt(xn, xn, cosw))
                tt(dst, xn, t, ALU.add).then_inc(done, 1)
                pool.wait_ge(done, count)

            nc.gpsimd.memset(gdT[:, :], 1.0).then_inc(s_set2, 1)
            nc.gpsimd.memset(reset[:, :], 1.0).then_inc(s_reset, 1)
            pool.wait_ge(s_reset, 1)
            nc.gpsimd.memset(reset[:, 0:T:GC], 0.0).then_inc(s_reset, 1)
            for step in SCHEDULE:
                kind = step[0]
                if kind == "xT":
                    pool.wait_ge(s_set, 2)
                    pool.wait_ge(s_mean, 1)
                    tt(rstd[:, 0:NB + 1], stat[:, 0:NB + 1], minus_half[:, 0:NB + 1], ALU.pow).then_inc(s_rstd, 1)
                    pool.wait_ge(s_const, CONST_DMAS * 16)
                    for i, (t, w) in enumerate((("cc", 0), ("ss", 1), ("cc", 2), ("ss", 3))):
                        tt(tab[:, i, :, :], C(t).rearrange("p (b d) -> p b d", d=DH),
                           qk_w[:, w:w + 1, :].to_broadcast([P, NB, DH]))
                    tt(tabm[:, 0, :], C("ccm", NM), qk_w[0:NM, 2, :])
                    link(tt(tabm[:, 1, :], C("ssm", NM), qk_w[0:NM, 3, :]))
                elif kind == "krope":
                    for b in range(NB):
                        pool.wait_ge(*banks.emptied(("unit", 5, b)))
                    pool.wait_ge(*banks.emptied(("unit", 5, "m")))
                    v = k_tok[:, :, :].rearrange("p b (g d) -> p (b g) d", d=DH)
                    rms(v, view(n_sq, P, 8), P, 8)
                    xn, t = view(n_x, P, 8), view(n_t, P, 8)
                    link(tt(xn, v, rstd[:, 0:8].unsqueeze(2).to_broadcast([P, 8, DH])))
                    hh = DH // 2
                    for g in range(HKV):
                        xh, th = (u.rearrange("p (b g) d -> p b g d", g=HKV)[:, :, g, :] for u in (xn, t))
                        tt(th[:, :, 0:hh], xh[:, :, hh:DH], tab[:, 3, :, 0:hh])
                        link(tt(th[:, :, hh:DH], xh[:, :, 0:hh], tab[:, 3, :, hh:DH]))
                        link(tt(xh, xh, tab[:, 2, :, :]))
                    tt(v, xn, t, ALU.add).then_inc(s_krope, 1)
                    pool.wait_ge(s_krope, 1)
                    m = km[:, 0:P].rearrange("p (g d) -> p g d", d=DH)
                    rope(m, tabm[:, 0:1, :].to_broadcast([NM, HKV, DH]), tabm[:, 1:2, :].to_broadcast([NM, HKV, DH]),
                         view(n_x, NM, HKV), view(n_sq, NM, HKV), krm[:, :].rearrange("p (g d) -> p g d", d=DH),
                         NM, HKV, s_krope, 2)
                elif kind == "qrope":
                    b = step[1]
                    pool.wait_ge(*banks.emptied(("unit", 6, b)))
                    pool.wait_ge(*banks.emptied(("unit", 7, b)))
                    q = q_tok[:, b, :].rearrange("p (g d) -> p g d", d=DH)
                    rope(q, tab[:, 0, b:b + 1, :].to_broadcast([P, HQ, DH]), tab[:, 1, b:b + 1, :].to_broadcast([P, HQ, DH]),
                         view(n_x, P, HQ), view(n_sq, P, HQ), q, P, HQ, s_qrope, b + 1)
                elif kind == "attT":
                    b = step[1]
                    if b == 0:
                        pool.wait_ge(s_gla_in, 5)
                        for t in att:
                            nc.gpsimd.memset(t[:, :, :], 0.0).then_inc(s_zero, 1)
                    pool.wait_ge(*banks.emptied(step))
                    nc.gpsimd.affine_select(out=att[b % 2][:, :, :], in_=att[b % 2][:, :, :], compare_op=ALU.is_ge,
                                            fill=0.0, base=0, pattern=[[0, GH], [1, P]], channel_multiplier=-1)\
                        .then_inc(s_attm, 1)
                elif kind == "unit" and CHUNKS[step[1]][0] == "rg":
                    _, c, u = step
                    pool.wait_ge(*banks.emptied(step))
                    r = rgs[:, u, (c - 8) * CW:(c - 7) * CW].rearrange("p (h v) -> p h v", v=GV)
                    link(tt(r, r, gla_w[:, :].unsqueeze(1).to_broadcast([P, 2, GV])))
                elif kind == "ognorm":
                    b = step[1]
                    pool.wait_ge(*banks.emptied(("glao", b)))
                    o = og[b][:, :].rearrange("p (h v) -> p h v", v=GV)
                    rms(og[b][:, :], n_sq[:, :], P, GH)
                    link(tt(o, o, rstd[:, 0:GH].unsqueeze(2).to_broadcast([P, GH, GV])))
                    tt(rgs[:, b, :], og[b][:, :], rgs[:, b, :]).then_inc(s_ogn, 1)
            pool.wait_ge(s_m2, 1)
            tt(rstd[:, 0:NB], stat[:, 0:NB], minus_half[:, 0:NB], ALU.pow).then_inc(s_r2, 1)

            pool.wait_ge(s_rounds, 1)
            pool.wait_ge(s_xs, 16 * NB)
            for b in range(NB):
                for half in range(2):
                    pool.wait_ge(*banks.filled(("nT", b, half)))
            rounds = pool.value_load(rounds_i[0:1, 0:1], min_val=1, max_val=T // SLOT)
            with pool.Fori(0, rounds) as r:
                with pool.Fori(0, PAIRS // 2) as i:
                    q = r * (PAIRS // 2) + i
                    for s in range(2):
                        pool.wait_ge(s_slots, r + 1)
                        pool.wait_ge(s_T, 2 * q + 1)
                        nc.gpsimd.tensor_copy(gather_i[s][:, :], slot_tok[:, bass.ds(2 * i + s, 1)]).then_inc(s_gidx, 1)
                        pool.wait_ge(s_gidx, 2 * q + s + 1)
                        nc.gpsimd.tensor_tensor(waited[:, s:s + 1], gather_i[s][:, :], gather_i[s][:, :], ALU.add)
                        nc.gpsimd.indirect_dma_start(
                            out=xg[s][:, :], out_offset=None, in_=xn_rows,
                            in_offset=bass.IndirectOffsetOnAxis(ap=gather_i[s][:, 0:1], axis=0)).then_inc(s_gath[s], 16)
                for s in range(2):
                    pool.wait_ge(s_rows, r + 1)
                    pool.wait_ge(s_yst[s], (r + 1) * (32 * PAIRS // 2) + 1)
                    nc.gpsimd.tensor_tensor(waited[:, 2 + s:3 + s], row_of[:, s, 0:1], row_of[:, s, 0:1], ALU.add)
                for b in range(NB):
                    for i in range(2):
                        nc.gpsimd.indirect_dma_start(
                            out=picked[2 * b + i][:, :], out_offset=None, in_=y_rows,
                            in_offset=bass.IndirectOffsetOnAxis(ap=row_of[:, i, b:b + 1], axis=0))\
                            .then_inc(s_pick[2 * b + i], 16)


_INS = ["x", "meta_tokens", "norm1_w", "w_in", "q_norm_w", "k_norm_w", "attn_sinks", "gla_gate_up", "gla_gate_bias",
        "gla_norm_w", "w_attn_branch", "w_gla_branch", "w_out", "norm2_w", "router_group", "router_expert",
        "expert_w_gate", "expert_w_up", "expert_w_down"]


def kernel(**inputs):
    import concourse.bacc as bacc
    from concourse.bass_utils import run_bass_kernel_spmd

    nc = bacc.Bacc("TRN2", target_bir_lowering=False, num_devices=1)
    arrays, args = {}, []
    for name in _INS:
        a = np.ascontiguousarray(inputs[name])
        arrays[f"in_{name}"] = a
        args.append(nc.dram_tensor(f"in_{name}", a.shape, mybir.dt.from_np(a.dtype), kind="ExternalInput").ap())
    table = shape_tables()
    arrays["table"] = table
    args.append(nc.dram_tensor("table", table.shape, F32, kind="ExternalInput").ap())
    args.append(nc.dram_tensor("xn_rows", (T, D), F32).ap())
    args.append(nc.dram_tensor("y_rows", (NE * SLOT, D), F32).ap())
    args.append(nc.dram_tensor("out", (1, T, D), F32, kind="ExternalOutput").ap())
    layer_kernel(nc, *args)
    r = run_bass_kernel_spmd(nc, [arrays], core_ids=[0])
    return r.results[0]["out"]
```

```python
from contextlib import ExitStack

import numpy as np
import concourse.bass as bass
from concourse import mybir

F32 = mybir.dt.float32
F32R = mybir.dt.float32r
U32 = mybir.dt.uint32
I32 = mybir.dt.int32
ALU = mybir.AluOpType
ACT = mybir.ActivationFunctionType
AX = mybir.AxisListType

D = 1024
T = 512
P = 128
NB = T // P
KT = D // P
NM = 16
XC = NM + T
HQ, HKV, DH = 8, 2, 64
GH, GK, GV = 4, 64, 128
GC = 64
NCH = T // GC
RANK = 16
NG, EPG, FF = 4, 8, 256
NE = NG * EPG
EPS = 1e-6
SCALE = DH ** -0.5
NEG = -1e30
CW = 256
SLOT = 64
PAIRS = NE // 2
BODIES = PAIRS // 2

GATHER_BANKS = (1, 0, 6, 7)
GU_BANK = (2, 0)
W_BANK = 1
H_BANK = (3, 2)
OH_BANK = (6, 7)
DOWN_BANKS = ((4, 5), (2, 1))
SCATTER_BANKS = (0, 6, 3, 7)

QA, KA, QG, KG, VG, RG, GD, GA, GG = 0, 512, 768, 1024, 1280, 1792, 2304, 2320, 3344

CST = {}
_o = 0
for _n, _w in (("ident", 128), ("mask", 272), ("cc", NB * DH), ("ss", NB * DH), ("ccm", DH), ("ssm", DH),
               ("slots", SLOT), ("tri", 128), ("gi", NG), ("ei", EPG)):
    CST[_n] = (_o, _o + _w)
    _o += _w
NCST = _o


def shape_tables():
    c = np.zeros((P, NCST), np.float32)

    def put(name, value):
        a, b = CST[name]
        c[:value.shape[0], a:b] = value.reshape(value.shape[0], -1)

    i, j = np.arange(P)[:, None], np.arange(P)[None, :]
    put("ident", np.eye(P, dtype=np.float32))
    prev = np.where(j > i, 0.0, NEG)
    own = np.where(j <= i, 0.0, NEG)
    put("mask", np.concatenate([prev, own, np.zeros((P, NM))], 1).astype(np.float32))
    half = DH // 2
    inv = np.float32(10000.0) ** (-(np.arange(half, dtype=np.float32) * np.float32(2.0)) / np.float32(DH))

    def angles(pos):
        a = pos.astype(np.float32)[..., None] * inv
        return (np.concatenate([np.cos(a), np.cos(a)], -1), np.concatenate([-np.sin(a), np.sin(a)], -1))

    cc, ss = angles(NM + np.arange(T).reshape(NB, P).T)
    put("cc", cc)
    put("ss", ss)
    cc, ss = angles(np.arange(NM))
    put("ccm", cc)
    put("ssm", ss)
    put("slots", np.tile(np.arange(SLOT, dtype=np.float32), (P, 1)))
    put("tri", (i < j).astype(np.float32))
    put("gi", np.tile(np.arange(NG, dtype=np.float32), (P, 1)))
    put("ei", np.tile(np.arange(EPG, dtype=np.float32), (P, 1)))
    return c


class Banks:

    def __init__(self, tiles, full, free, families):
        self.tiles, self.full, self.free, self.families = tiles, full, free, families
        self.uses = [0] * len(tiles)
        self.turn = {f: 0 for f in families}
        self.where = {}

    def take(self, pe, family, name):
        ring = self.families[family]
        b = ring[self.turn[family] % len(ring)]
        self.turn[family] += 1
        if self.uses[b]:
            pe.wait_ge(self.free[b], self.uses[b])
        self.uses[b] += 1
        self.where[name] = (b, self.uses[b])
        return self.tiles[b]

    def done(self, name):
        return self.full[self.where[name][0]]

    def filled(self, name):
        b, n = self.where[name]
        return self.full[b], n

    def get(self, name):
        return self.tiles[self.where[name][0]]

    def read(self, name):
        return self.free[self.where[name][0]]

    def emptied(self, name):
        b, n = self.where[name]
        return self.free[b], n


def weight_chunks():
    out = [("gd", GD, RANK, KT), ("qg", QG, CW, KT), ("kg", KG, CW, KT), ("vg", VG, CW, KT), ("vg", VG + CW, CW, KT),
           ("kva", KA, CW, KT), ("qa", QA, CW, KT), ("qa", QA + CW, CW, KT), ("rg", RG, CW, KT), ("rg", RG + CW, CW, KT)]
    for q in range(4):
        out += [("ga", GA + q * CW, CW, KT), ("gg", GG + q * CW, CW, KT)]
    for half in range(2):
        out += [("wg", half * 512, 512, 4), ("wa", half * 512, 512, 4)]
    out += [("wo", q * CW, CW, KT) for q in range(4)]
    return out


CHUNKS = weight_chunks()
NCHUNK = len(CHUNKS)
EARLY_DMAS = 2
CONST_DMAS = 18


def last_unit(c):
    kind = CHUNKS[c][0]
    if kind in ("gd", "kg", "vg", "kva"):
        return ("unit", c, "m")
    return ("unit", c, 1 if kind in ("qg", "ga", "gg") else 3)


def schedule():
    s = [("xT",), ("prep", 0), ("prep", 1)]
    s += [("unit", 0, 0), ("unit", 0, "m"), ("z",)]
    s += [("prep", 2), ("unit", 1, 0), ("unit", 1, 1)]
    s += [("prep", 3), ("unit", 2, 0), ("unit", 2, 1), ("unit", 2, "m")]
    s += [("prep", 4)] + [("unit", 3, 0), ("decay",)] + [("unit", 3, u) for u in (1, 2, 3, "m")]
    s += [("prep", 5)] + [("unit", 4, u) for u in (0, 1, 2, 3, "m")]
    s += [("prep", 6)] + [("unit", 5, u) for u in (0, 1, 2, 3, "m")] + [("krope",)]
    s += [("prep", 7), ("unit", 6, 0), ("kdm",), ("unit", 6, 1), ("kd", 0), ("kd", 1), ("kv", -1), ("unit", 6, 2),
          ("kd", 2), ("kd", 3), ("kv", 0), ("unit", 6, 3), ("kv", 1)]
    s += [("prep", 8)]
    for b in range(NB):
        s += [("unit", 7, b)]
        if b < 3:
            s += [("kv", 2 + b)]
        if b == 1:
            s += [("qrope", 0)]
    s += [("kv", 5), ("kv", 6), ("qrope", 1)]
    s += [("prep", 9)]
    for b in range(NB):
        s += [("unit", 8, b), ("attT", b)] + ([("kT",)] if b == 0 else [])
        if b == 1:
            s += [("qrope", 2)]
        if b >= 1:
            s += [("glao", b - 1)]
    s += [("qrope", 3)]
    s += [("prep", 10)]
    for b in range(NB):
        s += [("unit", 9, b)] + ([("glao", NB - 1)] if b == 0 else []) + [("qT", b), ("ognorm", b)]
    pairs = [(b, i) for b in range(NB) for i in range(4)]

    def product(n):
        b, i = pairs[n]
        return [("PV", b, i)] + ([("onorm", b)] if i == 3 else [])

    for c in range(10, 18):
        s += [("prep", c + 1)]
        for u in range(2):
            n = 2 * (c - 10) + u
            b, i = pairs[n]
            s += [("unit", c, u)] + (product(n - 2) if n >= 2 else [])
            s += [("S", b, i)] + ([("PT",) + pairs[n - 1]] if n >= 1 else [])
            if i == 2:
                s += [("ogT", b)] + ([("oT", b - 1)] if b >= 1 else [])
            s += [("sig", c, u)]
    s += [("prep", 19), ("unit", 18, 0)] + product(14) + [("PT",) + pairs[15], ("unit", 18, 1)] + product(15)
    s += [("unit", 18, 2), ("oT", NB - 1), ("unit", 18, 3)]
    for c in range(19, NCHUNK):
        s += [("prep", c + 1)] if c + 1 < NCHUNK else []
        s += [("unit", c, u) for u in range(4)]
    return s


SCHEDULE = schedule()


def layer_kernel(nc, x, meta_tokens, norm1_w, w_in, q_norm_w, k_norm_w, attn_sinks, gla_gate_up, gla_gate_bias,
                 gla_norm_w, w_attn_branch, w_gla_branch, w_out, norm2_w, router_group, router_expert,
                 expert_w_gate, expert_w_up, expert_w_down, table, out):
    with ExitStack() as ctx:
        def sb(name, shape, dt=F32):
            return ctx.enter_context(nc.sbuf_tensor(name, shape, dt))

        def sem(name):
            return ctx.enter_context(nc.semaphore(name))

        h = sb("h", [P, NB, D])
        cst = sb("cst", [P, NCST])
        norm1 = sb("norm1", [P, KT])
        norm2 = sb("norm2", [P, KT])
        qk_w = sb("qk_w", [P, 4, DH])
        gla_w = sb("gla_w", [P, GV])
        sinks = sb("sinks", [P, HQ])
        nsinks = sb("nsinks", [P, HQ])
        gate_up = sb("gate_up", [RANK + 1, GH * GK])
        router = sb("router", [P, KT, NG + NE])
        minus_half = sb("minus_half", [P, 16])
        ones = sb("ones", [P, P])
        stat = sb("stat", [P, 16])
        rstd = sb("rstd", [P, 16])

        def C(name, rows=P):
            a, b = CST[name]
            return cst[0:rows, a:b]

        ident = C("ident")

        arena_start = (nc.sbuf_base + 31) // 32 * 32
        arena_size = (nc.sbuf_usable_end - arena_start) // 32 * 32

        def at(name, offset, shape, dt=F32):
            size = int(np.prod(shape[1:])) * 4
            assert offset + size <= arena_size, (name, offset, size, arena_size)
            return nc.alloc_sbuf_tensor_at(name, shape, dt, offset=arena_start + offset)

        K1 = 1024
        wraw = [at(f"wraw{i}", i * 8 * K1, [P, KT * CW]) for i in range(2)]
        whi = [at(f"whi{i}", (16 + 8 * i) * K1, [P, KT * CW], F32R) for i in range(2)]
        wlo = [at(f"wlo{i}", (32 + 8 * i) * K1, [P, KT * CW], F32R) for i in range(2)]
        xhi = at("xhi", 48 * K1, [P, KT, XC], F32R)
        xlo = at("xlo", 48 * K1 + 16896, [P, KT, XC], F32R)
        mhi = at("mhi", 48 * K1, [P, KT, T], F32R)
        mlo = at("mlo", 64 * K1, [P, KT, T], F32R)
        G = 82 * K1
        g_b = at("g_b", G, [P, 2, T])
        g_d = at("g_d", G + 4 * K1, [P, 2, T])
        att = [at(f"att{i}", G + 2 * i * K1, [P, GH, P]) for i in range(2)]
        og = [at(f"og{i}", G + (24 + 2 * i) * K1, [P, 512]) for i in range(NB)]
        g_q1 = at("g_q1", G + 8 * K1, [P, 2, T])
        g_k1 = at("g_k1", G + 12 * K1, [P, 2, T])
        g_q3 = at("g_q3", G + 16 * K1, [P, 2, T])
        g_k4 = at("g_k4", G + 20 * K1, [P, 2, T])
        g_q = at("g_q", G + 24 * K1, [P, 2, T])
        g_k = at("g_k", G + 28 * K1, [P, 2, T])
        sig_a = at("sig_a", G, [P, KT, T])
        sig_g = at("sig_g", G + 16 * K1, [P, KT, T])
        vg = at("vg", G + 32 * K1, [P, NB, 512])
        kd = at("kd", G + 40 * K1, [P, NB, 256])
        st = at("st", G + 44 * K1, [P, NCH, 2, GV])
        ohi = at("ohi", G + 32 * K1, [P, 4, T], F32R)
        olo = at("olo", G + 40 * K1, [P, 4, T], F32R)
        rgs = at("rgs", G + 52 * K1, [P, NB, 512])
        tab = at("tab", G + 60 * K1, [P, 4, NB, DH])
        prob = [at(f"prob{i}", G + 60 * K1 + 1088 * i, [P, 272]) for i in range(4)]
        Q = G + 64 * K1 + 256
        qT = at("qT", Q, [P, 4, T])
        xm = at("xm", Q, [NM, D])
        xmf = at("xmf", Q + 4 * K1, [P, KT, NM])
        Y = Q + 8 * K1
        xr = at("xr", Y, [P, NB, D])
        q_tok = at("q_tok", Y, [P, NB, 512])
        n_sq = at("n_sq", Y + 8 * K1, [P, 512])
        n_x = at("n_x", Y + 10 * K1, [P, 512])
        n_t = at("n_t", Y + 12 * K1, [P, 512])
        vgm = at("vgm", Y + 14 * K1, [NM, 512])
        oghi = at("oghi", Y, [P, 4, T], F32R)
        oglo = at("oglo", Y + 8 * K1, [P, 4, T], F32R)
        ptm = [at(f"ptm{i}", 81 * K1 + 512 * i, [NM, P]) for i in range(2)]
        place = [Y + 16 * K1]

        def more(name, shape, dt=F32):
            t = at(name, place[0], shape, dt)
            place[0] += (int(np.prod(shape[1:])) * 4 + 31) // 32 * 32
            return t

        v_tok = more("v_tok", [P, NB, P])
        pt = [at(f"pt{i}", place[0] + K1 * i, [P, 256]) for i in range(2)]
        k_tok = more("k_tok", [P, NB, P])
        o_tok = at("o_tok", place[0], [P, 512])
        km = more("km", [NM, CW])
        kdm = more("kdm", [NM, CW])
        krm = more("krm", [NM, P])
        vm = more("vm", [NM, P])
        kT = more("kT", [P, XC])
        zm = more("zm", [P, 2, NM])
        lm = more("lm", [P, 2, NM])
        bm = more("bm", [P, 2, NM])
        kgm = more("kgm", [P, 2, NM])
        dec = more("dec", [P, 2 * NCH])
        tabm = more("tabm", [NM, 2, DH])
        att_stat = more("att_stat", [P, 2, 5, HQ])
        gdT = at("gdT", G + 64 * K1 + 256 + 4 * K1 + 512, [RANK + 1, XC])
        g_l = g_q1
        xj = at("xj", G + 32 * K1, [NM, D])
        reset = at("reset", Y + 16 * K1, [P, T])

        xs = at("xs", 0, [P, NB, D])
        xnT = at("xnT", 16 * K1, [P, KT, T])
        xs_hi = at("xs_hi", 32 * K1, [P, NB, D], F32R)
        xs_lo = at("xs_lo", 48 * K1, [P, NB, D], F32R)
        place = [64 * K1]
        logits = more("logits", [P, NB, NG + NE])
        g4 = [more(f"g4_{i}", [P, NB, NG]) for i in range(3)]
        e8 = [more(f"e8_{i}", [P, NB, EPG]) for i in range(6)]
        b4 = [more(f"b4_{i}", [P, NB]) for i in range(12)]
        first_e = more("first_e", [P, NB, NE])
        second_e = more("second_e", [P, NB, NE])
        chosen = more("chosen", [P, NB, NE])
        token_w = more("token_w", [P, NB, NE])
        rank = more("rank", [P, NB, NE + 4])
        r_tmp = more("r_tmp", [P, NB, NE])
        r_sel = more("r_sel", [P, NB, NE])
        counts = more("counts", [P, NE])
        n_round = more("n_round", [P, 4])
        rounds_i = more("rounds_i", [P, 1], I32)
        waited = more("waited", [P, 1])
        sums = [at("sums0", 30 * K1, [P, 512]), more("sums1", [P, 512])]
        pair_w = [more(f"pair_w{i}", [P, 1]) for i in range(2)]
        y_lo = [more(f"y_lo{i}", [P, D], F32R) for i in range(2)]
        assert place[0] <= 82 * K1, place[0] / K1
        onehot = at("onehot", 0, [P, NB, 2 * P], F32R)
        onehotT = [at(f"onehotT{i}", (4 + 2 * i) * K1, [P, NB, P], F32R) for i in range(2)]
        xgT = at("xgT", 8 * K1, [P, KT, 2 * P])
        hs = [at(f"hs{i}", (16 + i) * K1, [P, FF]) for i in range(2)]
        hg = [at(f"hg{i}", (18 + i) * K1, [P, FF]) for i in range(2)]
        hT = [at(f"hT{i}", (20 + i) * K1, [P, 2, P]) for i in range(2)]
        y_hi = [at(f"y_hi{i}", (22 + 4 * i) * K1, [P, D], F32R) for i in range(2)]
        we = [[[at(f"w{n}{s}{j}", 82 * K1 + (3 * (2 * s + j) + i) * 8 * K1, shape)
                for i, (n, shape) in enumerate((("gate", [P, KT, FF]), ("up", [P, KT, FF]), ("down", [P, 2, D])))]
               for j in range(2)] for s in range(2)]
        def view(t, rows, groups):
            return t[0:rows, 0:groups * DH].rearrange("p (g d) -> p g d", d=DH)

        tiles = [ctx.enter_context(nc.psum_tensor(f"bank{i}", [P, 512], F32)) for i in range(8)]
        banks = Banks(tiles, [sem(f"bank{i}_full") for i in range(8)], [sem(f"bank{i}_free") for i in range(8)],
                      {"unit": [0, 1, 2], "S": [3, 4], "T": [5, 6], "O": [7]})

        s_x = [sem(f"x{b}_loaded") for b in range(NB)]
        s_meta = sem("meta_loaded")
        s_early = sem("table_loaded")
        s_const = sem("constants_loaded")
        s_w = [sem(f"weights{i}_loaded") for i in range(2)]
        s_hi = sem("weights_hi")
        s_lo = sem("weights_lo")
        s_ones = sem("ones_set")
        s_out = sem("out_stored")
        s_set = sem("constants_set")
        s_set2 = sem("gate_rows_set")
        s_reset = sem("chunk_starts_set")
        s_sumsq = sem("x_squares_summed")
        s_mean = sem("x_means")
        s_rstd = sem("x_rstd")
        s_xr = sem("x_scaled")
        s_xhi = sem("xT_hi")
        s_xlo = sem("meta_xT_lo")
        s_l = sem("log_terms")
        s_diff = sem("decay_differences")
        s_exp = sem("decay_exps")
        s_gla_in = sem("gla_inputs")
        s_square = sem("norm_squares")
        s_mean2 = sem("norm_means")
        s_norm = sem("norm_rstd")
        s_krope = sem("k_roped")
        s_qrope = sem("q_roped")
        s_zero = sem("att_zeroed")
        s_attm = sem("att_masked")
        s_re = sem("rg_exp")
        s_ogn = sem("gla_out_normed")
        s_max = sem("score_max")
        s_prob = sem("probs_ready")
        s_es = sem("sink_terms")
        s_pv = sem("pv_done")
        s_ohi = sem("oT_hi")
        s_oghi = sem("ogT_hi")
        s_sig = sem("gates_ready")
        s_mer = sem("merged")
        s_mhi = sem("merged_hi")
        s_mlo = sem("merged_lo")
        s_pe = sem("tensor_chain")
        s_dve = sem("vector_chain")
        s_act = sem("scalar_chain")
        s_pool = sem("gpsimd_chain")

        s_xs_loc = sem("rows_scaled")
        s_sq2 = sem("residual_squares")
        s_m2 = sem("residual_means")
        s_r2 = sem("residual_rstd")
        s_xsh = sem("rows_hi")
        s_xsl = sem("rows_lo")
        s_rexp = sem("router_exps")
        s_rdiff = sem("router_differences")
        s_choice = sem("experts_chosen")
        s_rounds = sem("rounds_known")
        s_rank = sem("ranks_moved")

        def sem2(name):
            return [sem(f"{name}{i}") for i in range(2)]

        s_oh = sem("onehot_built")
        s_xg = [sem(f"rows{g}_gathered") for g in range(4)]
        s_xgT = [sem(f"rows{g}_weighted") for g in range(4)]
        s_padd = sem2("sums_added_by_gpsimd")
        s_pwm = sem("slot_weights_multiplied")
        s_pw = sem("slot_weights_ready")
        s_gu = sem2("gate_up_done")
        s_silu = sem2("silu_done")
        s_hg = sem2("hidden_ready")
        s_hTm = sem2("hidden_transposed")
        s_hT = sem2("hiddenT_ready")
        s_ohTm = sem2("onehot_transposed")
        s_ohT = sem2("onehotT_ready")
        s_down = sem2("down_done")
        s_yhi = sem2("y_hi_ready")
        s_ylo = sem2("y_lo_ready")
        s_wgu = sem2("gate_up_loaded")
        s_wd = sem2("down_loaded")
        s_sc = [sem(f"scatter_bank{i}_full") for i in range(4)]
        s_add = [sem(f"scatter_bank{i}_added") for i in range(4)]

        def w_source(c):
            kind, c0, n, kt = CHUNKS[c]
            if kind == "wa":
                return w_attn_branch[0, :, c0:c0 + n].rearrange("(k p) n -> p k n", p=P)
            if kind == "wg":
                return w_gla_branch[0, :, c0:c0 + n].rearrange("(k p) n -> p k n", p=P)
            if kind == "wo":
                return w_out[0, :, c0:c0 + n].rearrange("(k p) n -> p k n", p=P)
            return w_in[0, :, c0:c0 + n].rearrange("(p k) n -> p k n", k=KT)

        def w_view(t, c):
            kind, c0, n, kt = CHUNKS[c]
            return t[:, 0:kt * n].rearrange("p (k n) -> p k n", k=kt)

        def q_heads(b, g):
            return q_tok[:, b, :].rearrange("p (i g d) -> p g i d", g=2, d=DH)[:, g, :, :]

        def head_before(n, k):
            m = n - k
            return (m // 8, m % 8 // 2, m % 2)

        def chain(eng, s):
            count = [0]

            def link(ins):
                count[0] += 1
                ins.then_inc(s, 1)
                eng.wait_ge(s, count[0])
            return link

        def chunks_of(t):
            return t[:, :, :].rearrange("p j (c t) -> p (j c) t", t=GC)

        q0, k0 = q_norm_w[0, :], k_norm_w[0, :]
        hh = DH // 2
        consts = [(cst[:, :], table), (norm1[:, :], norm1_w[0].rearrange("(p k) -> p k", k=KT)),
                  (norm2[:, :], norm2_w[0].rearrange("(p k) -> p k", k=KT)),
                  (qk_w[:, 0, :], q0.partition_broadcast(P)),
                  (qk_w[:, 1, 0:hh], q0[hh:DH].partition_broadcast(P)),
                  (qk_w[:, 1, hh:DH], q0[0:hh].partition_broadcast(P)),
                  (qk_w[:, 2, :], k0.partition_broadcast(P)),
                  (qk_w[:, 3, 0:hh], k0[hh:DH].partition_broadcast(P)),
                  (qk_w[:, 3, hh:DH], k0[0:hh].partition_broadcast(P)),
                  (gla_w[:, :], gla_norm_w[0, :].partition_broadcast(P)),
                  (sinks[:, :], attn_sinks[0, :].partition_broadcast(P)),
                  (gate_up[0:RANK, :], gla_gate_up[0]), (gate_up[RANK:RANK + 1, :], gla_gate_bias),
                  (router[:, :, 0:NG], router_group[0].rearrange("(p k) g -> p k g", k=KT))]
        consts += [(router[:, :, NG + EPG * g:NG + EPG * (g + 1)],
                    router_expert[0, g].rearrange("(p k) e -> p k e", k=KT)) for g in range(NG)]
        assert len(consts) == CONST_DMAS

        block = ctx.enter_context(nc.Block())

        @block.tensor
        def _(pe):
            def mm3(ps, lhi, llo, rhi, rlo, kt, merged=False):
                for k in range(kt):
                    if merged:
                        pe.wait_ge(s_mlo, k + 1)
                    nc.tensor.matmul(ps, lhi(k), rhi(k), start=(k == 0), stop=False)
                    nc.tensor.matmul(ps, lhi(k), rlo(k), start=False, stop=False)
                    last = nc.tensor.matmul(ps, llo(k), rhi(k), start=False, stop=(k == kt - 1))
                return last

            link = chain(pe, s_pe)

            def cols(t, a, b):
                return lambda k: t[:, k, a:b]

            pe.wait_ge(s_early, EARLY_DMAS * 16)
            pe.wait_ge(s_ones, 1)
            for step in SCHEDULE:
                kind = step[0]
                if kind == "xT":
                    pe.wait_ge(s_xr, NB + 1)
                    for k in range(KT):
                        ps = banks.take(pe, "unit", ("xT", k))
                        for b in range(NB):
                            src = xr[:, b, :].rearrange("p (c k) -> p k c", k=KT)[:, k, :]
                            last = nc.tensor.transpose(ps[:, b * P:(b + 1) * P], src, ident)
                        last.then_inc(banks.done(("xT", k)), 1)
                    ps = banks.take(pe, "T", "xmT")
                    for k in range(KT):
                        src = xm[:, :].rearrange("p (c k) -> p k c", k=KT)[:, k, :]
                        last = nc.tensor.transpose(ps[:, k * NM:(k + 1) * NM], src, ident[0:NM, 0:NM])
                    last.then_inc(banks.done("xmT"), 1)
                elif kind == "unit":
                    _, c, u = step
                    name, c0, n, kt = CHUNKS[c]
                    if u == 0:
                        pe.wait_ge(s_lo, c + 1)
                    if c == 0 and u == 0:
                        for k in range(KT - 3, KT):
                            pe.wait_ge(*banks.emptied(("xT", k)))
                        pe.wait_ge(s_xlo, 1)
                    wh, wl = w_view(whi[c % 2], c), w_view(wlo[c % 2], c)
                    meta = u == "m"
                    xa, xb = (0, NM) if meta else (NM, XC)
                    if name in ("qg", "kg", "gd", "ga", "gg"):
                        if meta and name == "kg":
                            ps = banks.take(pe, "unit", step)
                            for j in range(2):
                                last = mm3(ps[:, j * NM:(j + 1) * NM], cols(wh, j * P, (j + 1) * P),
                                           cols(wl, j * P, (j + 1) * P), cols(xhi, xa, xb), cols(xlo, xa, xb), KT)
                        else:
                            ps = banks.take(pe, "unit", step)
                            a, b = (0, RANK) if name == "gd" else (u * P, (u + 1) * P)
                            last = mm3(ps[0:b - a, 0:xb - xa], cols(wh, a, b), cols(wl, a, b),
                                       cols(xhi, xa, xb), cols(xlo, xa, xb), KT)
                    elif name in ("vg", "kva", "qa", "rg"):
                        ps = banks.take(pe, "unit", step)
                        a, b = (0, NM) if meta else (NM + u * P, NM + (u + 1) * P)
                        last = mm3(ps[0:b - a, 0:n], cols(xhi, a, b), cols(xlo, a, b), cols(wh, 0, n), cols(wl, 0, n), KT)
                    elif name in ("wa", "wg"):
                        if u == 0 and c0 == 0:
                            for b in range(NB):
                                pe.wait_ge(*banks.emptied(("ogT" if name == "wg" else "oT", b)))
                        ih, il = (oghi, oglo) if name == "wg" else (ohi, olo)
                        ps = banks.take(pe, "unit", step)
                        last = mm3(ps[:, :], cols(wh, u * P, (u + 1) * P), cols(wl, u * P, (u + 1) * P),
                                   cols(ih, 0, T), cols(il, 0, T), 4)
                    else:
                        ps = banks.take(pe, "unit", step)
                        last = mm3(ps[:, 0:n], cols(mhi, u * P, (u + 1) * P), cols(mlo, u * P, (u + 1) * P),
                                   cols(wh, 0, n), cols(wl, 0, n), KT, merged=(c0 == 0 and u == 0))
                    last.then_inc(banks.done(step), 1)
                elif kind == "z":
                    pe.wait_ge(s_const, (CONST_DMAS - EARLY_DMAS) * 16)
                    pe.wait_ge(*banks.emptied(("unit", 0, 0)))
                    pe.wait_ge(*banks.emptied(("unit", 0, "m")))
                    for j in range(2):
                        ps = banks.take(pe, "unit", ("z", j))
                        nc.tensor.matmul(ps[:, :], gate_up[:, j * P:(j + 1) * P], gdT[:, NM:XC],
                                         start=True, stop=True).then_inc(banks.done(("z", j)), 1)
                    ps = banks.take(pe, "T", "zm")
                    for j in range(2):
                        last = nc.tensor.matmul(ps[:, j * NM:(j + 1) * NM], gate_up[:, j * P:(j + 1) * P],
                                                gdT[:, 0:NM], start=True, stop=True)
                    last.then_inc(banks.done("zm"), 1)
                elif kind == "kdm":
                    pe.wait_ge(s_gla_in, 5)
                    ps = banks.take(pe, "T", "kdm")
                    for j in range(2):
                        last = nc.tensor.transpose(ps[0:NM, j * P:(j + 1) * P], kgm[:, j, :], ident)
                    last.then_inc(banks.done("kdm"), 1)
                elif kind == "kd":
                    b = step[1]
                    ps = banks.take(pe, "T", step)
                    for j in range(2):
                        last = nc.tensor.transpose(ps[:, j * P:(j + 1) * P], g_k4[:, j, b * P:(b + 1) * P], ident)
                    last.then_inc(banks.done(step), 1)
                elif kind == "kv":
                    c = step[1]
                    ps = banks.take(pe, "S", step)
                    if c < 0:
                        pe.wait_ge(*banks.emptied("kdm"))
                        pe.wait_ge(*banks.emptied(("unit", 3, "m")))
                        pe.wait_ge(*banks.emptied(("unit", 4, "m")))
                    else:
                        pe.wait_ge(*banks.emptied(("kd", c // 2)))
                    for hd in range(GH):
                        a = (hd % 2) * GK
                        o = ps[a:a + GK, (hd // 2) * GV:(hd // 2 + 1) * GV]
                        if c < 0:
                            lhs, rhs = kdm[:, hd * GK:(hd + 1) * GK], vgm[:, hd * GV:(hd + 1) * GV]
                        else:
                            t0 = (c % 2) * GC
                            lhs = kd[t0:t0 + GC, c // 2, hd * GK:(hd + 1) * GK]
                            rhs = vg[t0:t0 + GC, c // 2, hd * GV:(hd + 1) * GV]
                        last = nc.tensor.matmul(o, lhs, rhs, start=True, stop=True)
                    last.then_inc(banks.done(step), 1)
                elif kind == "attT":
                    b = step[1]
                    ps = banks.take(pe, "S", step)
                    for hd in (0, 2, 1, 3):
                        a = (hd % 2) * GK
                        last = nc.tensor.matmul(ps[:, hd * P:(hd + 1) * P],
                                                g_k1[a:a + GK, hd // 2, b * P:(b + 1) * P],
                                                g_q1[a:a + GK, hd // 2, b * P:(b + 1) * P], start=True, stop=True)
                        if hd == 2:
                            link(last)
                    last.then_inc(banks.done(step), 1)
                elif kind == "glao":
                    b = step[1]
                    ps = banks.take(pe, "O", step)
                    pe.wait_ge(s_attm, b + 1)
                    pe.wait_ge(*banks.emptied(("kv", 2 * b)))
                    for hd in (0, 2, 1, 3):
                        a = (hd % 2) * GK
                        o = ps[:, hd * GV:(hd + 1) * GV]
                        nc.tensor.matmul(o, att[b % 2][:, hd, :], vg[:, b, hd * GV:(hd + 1) * GV],
                                         start=True, stop=False)
                        for s in range(2):
                            t0 = b * P + s * GC
                            last = nc.tensor.matmul(ps[s * GC:(s + 1) * GC, hd * GV:(hd + 1) * GV],
                                                    g_q3[a:a + GK, hd // 2, t0:t0 + GC],
                                                    st[a:a + GK, 2 * b + s, hd // 2, :],
                                                    start=False, stop=True)
                        if hd == 2:
                            link(last)
                    last.then_inc(banks.done(step), 1)
                elif kind == "kT":
                    pe.wait_ge(s_krope, 2)
                    ps = banks.take(pe, "T", "kT")
                    for b in range(NB):
                        last = nc.tensor.transpose(ps[:, b * P:(b + 1) * P], k_tok[:, b, :], ident)
                    last.then_inc(banks.done("kT"), 1)
                    ps = banks.take(pe, "T", "kTm")
                    nc.tensor.transpose(ps[:, 0:NM], krm[:, :], ident[0:NM, 0:NM]).then_inc(banks.done("kTm"), 1)
                elif kind == "qT":
                    b = step[1]
                    pe.wait_ge(s_qrope, b + 1)
                    ps = banks.take(pe, "T", step)
                    for i in range(4):
                        last = nc.tensor.transpose(ps[:, i * P:(i + 1) * P], q_tok[:, b, i * P:(i + 1) * P], ident)
                    last.then_inc(banks.done(step), 1)
                elif kind == "S":
                    _, b, i = step
                    if i == 0:
                        pe.wait_ge(*banks.emptied(("qT", b)))
                    if i == 0 and b == 0:
                        pe.wait_ge(*banks.emptied("kT"))
                        pe.wait_ge(*banks.emptied("kTm"))
                    for j in range(2):
                        ps = banks.take(pe, "S", ("S", b, i, j))
                        q = qT[j * DH:(j + 1) * DH, i, b * P:(b + 1) * P]
                        if b == 0:
                            nc.tensor.matmul(ps[:, 128:256], q, kT[j * DH:(j + 1) * DH, NM:NM + P], start=True, stop=True)
                        else:
                            nc.tensor.matmul(ps[:, 0:256], q, kT[j * DH:(j + 1) * DH, NM + (b - 1) * P:NM + (b + 1) * P],
                                             start=True, stop=True)
                        nc.tensor.matmul(ps[:, 256:272], q, kT[j * DH:(j + 1) * DH, 0:NM],
                                         start=True, stop=True).then_inc(banks.done(("S", b, i, j)), 1)
                elif kind == "PT":
                    _, b, i = step
                    n0 = 2 * (4 * b + i)
                    for j in range(2):
                        pe.wait_ge(s_prob, n0 + j + 1)
                        ps = banks.take(pe, "T", ("PT", b, i, j))
                        p = prob[(n0 + j) % 4]
                        if b > 0:
                            nc.tensor.transpose(ps[:, 0:128], p[:, 0:128], ident)
                        nc.tensor.transpose(ps[:, 128:256], p[:, 128:256], ident)
                        nc.tensor.transpose(ps[0:NM, 256:384], p[:, 256:272], ident).then_inc(banks.done(("PT", b, i, j)), 1)
                elif kind == "PV":
                    _, b, i = step
                    if i == 0:
                        pv = banks.take(pe, "O", ("PV", b))
                    for j in range(2):
                        pe.wait_ge(*banks.emptied(("PT", b, i, j)))
                        hd = j * 4 + i
                        o = pv[:, hd * DH:(hd + 1) * DH]
                        vc = slice(j * DH, (j + 1) * DH)
                        if b > 0:
                            nc.tensor.matmul(o, pt[j][:, 0:128], v_tok[:, b - 1, vc], start=True, stop=False)
                        nc.tensor.matmul(o, pt[j][:, 128:256], v_tok[:, b, vc], start=(b == 0), stop=False)
                        last = nc.tensor.matmul(o, ptm[j][:, :], vm[:, vc],
                                                start=False, stop=True)
                    last.then_inc(s_pv, 1)
                elif kind in ("oT", "ogT"):
                    b = step[1]
                    if kind == "oT":
                        pe.wait_ge(*banks.emptied(("PV", b)))
                    else:
                        pe.wait_ge(s_ogn, b + 1)
                    src = o_tok[:, :] if kind == "oT" else rgs[:, b, :]
                    ps = banks.take(pe, "T", step)
                    for j in range(4):
                        last = nc.tensor.transpose(ps[:, j * P:(j + 1) * P], src[:, j * P:(j + 1) * P], ident)
                    last.then_inc(banks.done(step), 1)

            def row_transposes(b):
                pe.wait_ge(s_xs_loc, b + 1)
                for half in range(2):
                    ps = banks.take(pe, "unit", ("nT", b, half))
                    for k in range(4):
                        src = xs[:, b, :].rearrange("p (c k) -> p k c", k=KT)[:, 4 * half + k, :]
                        last = nc.tensor.transpose(ps[:, k * P:(k + 1) * P], src, ident)
                    last.then_inc(banks.done(("nT", b, half)), 1)

            row_transposes(0)
            for b in range(NB):
                if b + 1 < NB:
                    row_transposes(b + 1)
                ps = banks.take(pe, "S", ("logit", b))
                for half in range(2):
                    pe.wait_ge(*banks.emptied(("nT", b, half)))
                    for k in range(4 * half, 4 * half + 4):
                        last = nc.tensor.matmul(ps[:, 0:NG + NE], xnT[:, k, b * P:(b + 1) * P], router[:, k, :],
                                                start=(k == 0), stop=(k == KT - 1))
                last.then_inc(banks.done(("logit", b)), 1)
            pe.wait_ge(s_choice, 1)
            ps = banks.take(pe, "S", "rank")
            for b in range(NB + 1):
                for b2 in range(min(b + 1, NB)):
                    last = nc.tensor.matmul(ps[:, b * NE:(b + 1) * NE], C("tri") if b2 == b else ones[:, :],
                                            chosen[:, b2, :], start=(b2 == 0), stop=(b2 == min(b, NB - 1)))
            last.then_inc(banks.done("rank"), 1)

            pe.wait_ge(*banks.emptied("rank"))
            pe.wait_ge(s_rounds, 1)
            rounds = pe.value_load(rounds_i[0:1, 0:1], min_val=1, max_val=T // SLOT)
            for b in range(NB):
                for half in range(2):
                    pe.wait_ge(*banks.emptied(("nT", b, half)))
            pe.wait_ge(s_xsl, NB)
            with pe.Fori(0, rounds) as r:
                with pe.Fori(0, BODIES) as i:
                    n = r * BODIES + i

                    def oh(s, b):
                        return onehot[:, b, s * P:(s + 1) * P].bitcast(F32)

                    pe.wait_ge(s_oh, r * (BODIES + 1) + i + 1)
                    for g, bank in enumerate(GATHER_BANKS):
                        if bank in SCATTER_BANKS:
                            pe.wait_ge(s_add[SCATTER_BANKS.index(bank)], 4 * n + 1)
                        for k in range(2):
                            for b in range(NB):
                                for part in (xs_hi, xs_lo):
                                    lhs = part[:, b, :].rearrange("p (c k) -> p k c", k=KT)[:, 2 * g + k, :]
                                    last = nc.tensor.matmul(tiles[bank][:, k * 2 * P:(k + 1) * 2 * P], lhs, onehot[:, b, :],
                                                            start=(b == 0 and part is xs_hi),
                                                            stop=(b == NB - 1 and part is xs_lo))
                        last.then_inc(s_xg[g], 1)
                    pe.wait_ge(s_xgT[0], n + 1)
                    for s in range(2):
                        for b in range(NB):
                            last = nc.tensor.matmul(tiles[W_BANK][:, 2 * s:2 * s + 2], oh(s, b),
                                                    token_w[:, b, bass.ds(4 * i + 2 * s, 2)],
                                                    start=(b == 0), stop=(b == NB - 1))
                    last.then_inc(s_pwm, 1)
                    for s in range(2):
                        if s == 0:
                            for g in range(1, 4):
                                pe.wait_ge(s_xgT[g], n + 1)
                        pe.wait_ge(s_wgu[s], 64 * n + 64)
                        for f in range(2):
                            for k in range(KT):
                                for j in range(2):
                                    last = nc.tensor.matmul(tiles[GU_BANK[s]][j * SLOT:(j + 1) * SLOT, f * FF:(f + 1) * FF],
                                                            xgT[:, k, s * P + j * SLOT:s * P + (j + 1) * SLOT], we[s][j][f][:, k, :],
                                                            start=(k == 0), stop=(k == KT - 1))
                        last.then_inc(s_gu[s], 1)

                    def hidden_transposes(s):
                        pe.wait_ge(s_hg[s], n + 1)
                        for f in range(2):
                            last = nc.tensor.transpose(tiles[H_BANK[s]][:, f * P:(f + 1) * P],
                                                       hg[s][:, f * P:(f + 1) * P], ident)
                        last.then_inc(s_hTm[s], 1)

                    pe.wait_ge(s_add[SCATTER_BANKS.index(H_BANK[0])], 4 * n + 1)
                    hidden_transposes(0)
                    for s in range(2):
                        for b in range(NB):
                            last = nc.tensor.transpose(tiles[OH_BANK[s]][:, b * P:(b + 1) * P],
                                                       oh(s, b), ident)
                        last.then_inc(s_ohTm[s], 1)
                    hidden_transposes(1)
                    for s in range(2):
                        pe.wait_ge(s_hT[s], n + 1)
                        pe.wait_ge(s_wd[s], 32 * n + 32)
                        if s:
                            pe.wait_ge(s_pw, n + 1)
                        for half in range(2):
                            for f in range(2):
                                for j in range(2):
                                    last = nc.tensor.matmul(tiles[DOWN_BANKS[s][half]][j * SLOT:(j + 1) * SLOT, :],
                                                            hT[s][:, f, j * SLOT:(j + 1) * SLOT],
                                                            we[s][j][2][:, f, half * 512:(half + 1) * 512],
                                                            start=(f == 0), stop=(f == 1))
                        last.then_inc(s_down[s], 1)
                    for u in range(16):
                        s, b, half = u // 8, u % 8 // 2, u % 2
                        if u % 8 == 0:
                            pe.wait_ge(s_ohT[1], n + 1)
                            pe.wait_ge(s_ylo[s], n + 1)
                        if u >= 4:
                            pe.wait_ge(s_add[u % 4], 4 * n + u // 4 + 1)
                        cols_ = slice(half * 512, (half + 1) * 512)
                        nc.tensor.matmul(tiles[SCATTER_BANKS[u % 4]][:, :], onehotT[s][:, b, :], y_hi[s][:, cols_],
                                         start=True, stop=False)
                        nc.tensor.matmul(tiles[SCATTER_BANKS[u % 4]][:, :], onehotT[s][:, b, :], y_lo[s][:, cols_],
                                         start=False, stop=True).then_inc(s_sc[u % 4], 1)

        @block.sync
        def _(sp):
            def load_w(c):
                if c >= 2:
                    sp.wait_ge(s_lo, c - 1)
                sp.dma_start(w_view(wraw[c % 2], c), w_source(c)).then_inc(s_w[c % 2], 16)

            for started in (s_rank, *s_add, *s_padd):
                sp.sem_inc(started, 1)
            for b in range(NB):
                sp.dma_start(h[:, b, :], x[0, b * P:(b + 1) * P, :]).then_inc(s_x[b], 16)
            sp.dma_start(xm[:, :], meta_tokens).then_inc(s_meta, 16)
            for c in range(2):
                load_w(c)
            for dst, src in consts[EARLY_DMAS:]:
                sp.dma_start(dst, src).then_inc(s_const, 16)
            for c in range(2, NCHUNK):
                load_w(c)

            def load(pair, s, gate_up):
                for j in range(2):
                    e = pair * 2 + j
                    for i, w in ((0, expert_w_gate), (1, expert_w_up)) if gate_up else ((2, expert_w_down),):
                        src = w[0].rearrange("g e a n -> (g e) a n")[bass.ds(e, 1), :, :]
                        src = src.rearrange("o (p k) n -> p (o k) n", p=P) if gate_up else \
                            src.rearrange("o (k p) n -> p (o k) n", p=P)
                        sp.dma_start(we[s][j][i][:, :, :], src).then_inc((s_wgu if gate_up else s_wd)[s], 16)

            def reload(i, n):
                for s in range(2):
                    sp.wait_ge(s_gu[s], n)
                    load(2 * i + s, s, True)
                for s in range(2):
                    sp.wait_ge(s_down[s], n)
                    load(2 * i + s, s, False)

            sp.wait_ge(s_mlo, KT)
            for s in range(2):
                load(s, s, True)
                load(s, s, False)
            with sp.Fori(1, BODIES) as i:
                reload(i, i)
            sp.wait_ge(s_rounds, 1)
            rounds = sp.value_load(rounds_i[0:1, 0:1], min_val=1, max_val=T // SLOT)
            with sp.If(rounds > 1):
                with sp.Fori(1, rounds) as r:
                    with sp.Fori(0, BODIES) as i:
                        reload(i, r * BODIES + i)
            for added in s_add:
                sp.wait_ge(added, rounds * (4 * BODIES) + 1)
            for added in s_padd:
                sp.wait_ge(added, rounds * (2 * BODIES) + 1)
            for b in range(NB):
                sp.dma_start(out[0, b * P:(b + 1) * P, :], h[:, b, :]).then_inc(s_out, 16)
            sp.wait_ge(s_out, 16 * NB)

        @block.scalar
        def _(act):
            link = chain(act, s_act)
            for dst, src in consts[:EARLY_DMAS]:
                act.dma_start(dst, src).then_inc(s_early, 16)

            norms = [0]

            def squares(src, rows, width):
                if norms[0]:
                    act.wait_ge(s_mean2, norms[0])
                norms[0] += 1
                nc.scalar.activation(n_sq[0:rows, 0:width], src, ACT.Square).then_inc(s_square, 1)

            for step in SCHEDULE:
                kind = step[0]
                if kind == "prep":
                    c = step[1]
                    act.wait_ge(s_w[c % 2], 16 * (c // 2 + 1))
                    if c >= 2:
                        act.wait_ge(*banks.filled(last_unit(c - 2)))
                    nc.scalar.activation(w_view(whi[c % 2], c), w_view(wraw[c % 2], c), ACT.Copy).then_inc(s_hi, 1)
                elif kind == "krope":
                    for u in (0, 1, 2, 3, "m"):
                        act.wait_ge(*banks.emptied(("unit", 5, u)))
                    squares(k_tok[:, :, :].rearrange("p b c -> p (b c)"), P, NB * P)
                    squares(km[:, 0:P], NM, P)
                elif kind == "qrope":
                    b = step[1]
                    act.wait_ge(*banks.emptied(("unit", 6, b)))
                    act.wait_ge(*banks.emptied(("unit", 7, b)))
                    squares(q_tok[:, b, :], P, 512)
                elif kind == "ognorm":
                    b = step[1]
                    act.wait_ge(*banks.emptied(("glao", b)))
                    squares(og[b][:, :], P, 512)
                elif kind == "xT":
                    act.wait_ge(s_set, 2)
                    for b in range(NB):
                        act.wait_ge(s_x[b], 16)
                        nc.scalar.activation(xr[:, b, :], h[:, b, :], ACT.Square,
                                             accum_out=stat[:, b:b + 1]).then_inc(s_sumsq, 1)
                    act.wait_ge(s_meta, 16)
                    nc.scalar.activation(xj[:, :], xm[:, :], ACT.Square,
                                         accum_out=stat[0:NM, NB:NB + 1]).then_inc(s_sumsq, 1)
                    act.wait_ge(s_early, EARLY_DMAS * 16)
                    for k in range(KT):
                        act.wait_ge(*banks.filled(("xT", k)))
                        nc.scalar.activation(xhi[:, k, NM:XC], banks.get(("xT", k))[:, :], ACT.Copy,
                                             scale=norm1[:, k:k + 1]).then_inc(s_xhi, 1)
                    act.wait_ge(*banks.emptied("xmT"))
                    nc.scalar.activation(xhi[:, :, 0:NM], xmf[:, :, :], ACT.Copy).then_inc(s_xhi, 1)
                elif kind == "unit":
                    _, c, u = step
                    name, c0, n, kt = CHUNKS[c]
                    if name == "wa":
                        j = c0 // P + u
                        act.wait_ge(s_mer, j + 1)
                        nc.scalar.activation(mhi[:, j, :], sig_a[:, j, :], ACT.Copy).then_inc(s_mhi, 1)
                        continue
                    if name == "vg" and c == 4 or name == "qa" and c == 7 or name in ("wg", "wo"):
                        continue
                    if name in ("ga", "gg") and (c, u) == (10, 0):
                        act.wait_ge(*banks.filled(("glao", NB - 1)))
                    if (c, u) == (11, 0):
                        act.wait_ge(s_ogn, NB)
                    act.wait_ge(*banks.filled(step))
                    ps = banks.get(step)
                    if name == "gd":
                        act.wait_ge(s_set2, 1)
                        dst, src = (gdT[0:RANK, NM:XC], ps[0:RANK, :]) if u == 0 else (gdT[0:RANK, 0:NM], ps[0:RANK, 0:NM])
                        nc.scalar.activation(dst, src, ACT.Copy).then_inc(banks.read(step), 1)
                    elif name == "qg":
                        nc.scalar.activation(g_q[:, u, :], ps[:, :], ACT.Copy, scale=GK ** -0.5).then_inc(banks.read(step), 1)
                    elif name == "kg" and u != "m":
                        nc.scalar.activation(g_k[:, u, :], ps[:, :], ACT.Copy).then_inc(banks.read(step), 1)
                    elif name == "kg":
                        nc.scalar.activation(kgm[:, :, :], ps[:, 0:2 * NM], ACT.Copy).then_inc(banks.read(step), 1)
                    elif name == "vg":
                        dst = vgm[:, 0:CW] if u == "m" else vg[:, u, 0:CW]
                        nc.scalar.activation(dst, ps[0:NM if u == "m" else P, 0:CW], ACT.Copy).then_inc(banks.read(step), 1)
                    elif name == "kva":
                        kd_, vd_, r = (km[:, 0:P], vm[:, :], NM) if u == "m" else (k_tok[:, u, :], v_tok[:, u, :], P)
                        nc.scalar.activation(kd_, ps[0:r, 0:P], ACT.Copy)
                        nc.scalar.activation(vd_, ps[0:r, P:2 * P], ACT.Copy).then_inc(banks.read(step), 1)
                    elif name == "qa":
                        nc.scalar.activation(q_heads(u, 0), ps[:, 0:CW].rearrange("p (i d) -> p i d", d=DH), ACT.Copy).then_inc(banks.read(step), 1)
                    elif name == "rg":
                        o = (c - 8) * CW
                        nc.scalar.activation(rgs[:, u, o:o + CW], ps[:, 0:CW], ACT.Exp, scale=-1.0).then_inc(s_re, 1)
                    else:
                        j = (c - 10) // 2 * 2 + u
                        dst = sig_a if name == "ga" else sig_g
                        nc.scalar.activation(dst[:, j, :], ps[:, :], ACT.Exp, scale=-1.0).then_inc(banks.read(step), 1)
                elif kind == "z":
                    act.wait_ge(s_const, (CONST_DMAS - EARLY_DMAS) * 16)
                    for j in range(3):
                        act.wait_ge(*banks.emptied(("z", j) if j < 2 else "zm"))
                        dst, src = (g_l[:, j, :], g_d[:, j, :]) if j < 2 else (lm[:, :, :], zm[:, :, :])
                        link(nc.scalar.activation(dst, src, ACT.Exp, scale=-1.0))
                    for j in range(3):
                        dst = g_l[:, j, :] if j < 2 else lm[:, :, :]
                        nc.scalar.activation(dst, dst, ACT.Ln, bias=1.0).then_inc(s_l, 1)
                elif kind == "decay":
                    s = 1.0 / 16.0
                    act.wait_ge(s_diff, 1)
                    nc.scalar.activation(g_q1[:, :, :], g_d[:, :, :], ACT.Exp, scale=s).then_inc(s_exp, 1)
                    nc.scalar.activation(g_k1[:, :, :], g_d[:, :, :], ACT.Exp, scale=-s).then_inc(s_exp, 1)
                    nc.scalar.activation(g_q3[:, :, :], g_b[:, :, :], ACT.Exp, scale=s).then_inc(s_exp, 1)
                    act.wait_ge(s_diff, 2)
                    nc.scalar.activation(g_k4[:, :, :], g_k4[:, :, :], ACT.Exp, scale=s).then_inc(s_exp, 1)
                    act.wait_ge(s_diff, 3)
                    nc.scalar.activation(lm[:, :, :], lm[:, :, :], ACT.Exp, scale=s).then_inc(s_exp, 1)
                    nc.scalar.activation(dec[:, :], chunks_of(g_b)[:, :, GC - 1], ACT.Exp, scale=s).then_inc(s_exp, 1)
                elif kind == "attT":
                    b = step[1]
                    act.wait_ge(*banks.filled(step))
                    act.wait_ge(s_zero, 2)
                    if b >= 2:
                        act.wait_ge(*banks.filled(("glao", b - 2)))
                    ps = banks.get(step)[:, :].rearrange("p (h i) -> p h i", h=GH)
                    nc.scalar.activation(att[b % 2][0:GC, :, 0:GC], ps[0:GC, :, 0:GC], ACT.Copy)
                    nc.scalar.activation(att[b % 2][GC:P, :, GC:P], ps[GC:P, :, GC:P], ACT.Copy).then_inc(banks.read(step), 1)
                elif kind == "glao":
                    b = step[1]
                    act.wait_ge(*banks.filled(step))
                    nc.scalar.activation(og[b][:, :], banks.get(step)[:, :], ACT.Copy).then_inc(banks.read(step), 1)
                elif kind == "kT":
                    act.wait_ge(*banks.filled("kT"))
                    nc.scalar.activation(kT[:, NM:XC], banks.get("kT")[:, :], ACT.Copy).then_inc(banks.read("kT"), 1)
                    act.wait_ge(*banks.filled("kTm"))
                    nc.scalar.activation(kT[:, 0:NM], banks.get("kTm")[:, 0:NM], ACT.Copy).then_inc(banks.read("kTm"), 1)
                elif kind == "qT":
                    b = step[1]
                    act.wait_ge(*banks.filled(step))
                    ps = banks.get(step)[:, :].rearrange("p (i t) -> p i t", i=4)
                    nc.scalar.activation(qT[:, :, b * P:(b + 1) * P], ps, ACT.Copy).then_inc(banks.read(step), 1)
                elif kind == "S":
                    _, b, i = step
                    for j in range(2):
                        n = 2 * (4 * b + i) + j
                        hd = j * 4 + i
                        act.wait_ge(s_max, n + 1)
                        st_ = att_stat[:, b % 2, :, hd:hd + 1]
                        p = prob[n % 4][:, 128 if b == 0 else 0:272]
                        nc.scalar.activation(p, p, ACT.Exp, bias=st_[:, 1, :], scale=SCALE,
                                             accum_out=st_[:, 2, :]).then_inc(s_prob, 1)
                        nc.scalar.activation(st_[:, 3, :], sinks[:, hd:hd + 1], ACT.Exp,
                                             bias=st_[:, 1, :]).then_inc(s_es, 1)
                elif kind == "PT":
                    _, b, i = step
                    name = ("PT", b, i, 0)
                    act.wait_ge(*banks.filled(name))
                    if 4 * b + i:
                        act.wait_ge(s_pv, 4 * b + i)
                    ps = banks.get(name)
                    c0 = 128 if b == 0 else 0
                    nc.scalar.activation(pt[0][:, c0:256], ps[:, c0:256], ACT.Copy)
                    nc.scalar.activation(ptm[0][:, :], ps[0:NM, 256:384], ACT.Copy).then_inc(banks.read(name), 1)
                elif kind in ("oT", "ogT"):
                    b = step[1]
                    act.wait_ge(*banks.filled(step))
                    dst, s = (ohi, s_ohi) if kind == "oT" else (oghi, s_oghi)
                    ps = banks.get(step)[:, :].rearrange("p (j t) -> p j t", j=4)
                    nc.scalar.activation(dst[:, :, b * P:(b + 1) * P], ps, ACT.Copy).then_inc(s, 1)

            for b in range(NB):
                for c in range(22, 26):
                    act.wait_ge(*banks.emptied(("unit", c, b)))
                nc.scalar.activation(xs[:, b, :], h[:, b, :], ACT.Square, accum_out=stat[:, b:b + 1]).then_inc(s_sq2, 1)
            for b in range(NB):
                act.wait_ge(s_xs_loc, b + 1)
                nc.scalar.activation(xs_hi[:, b, :], xs[:, b, :], ACT.Copy).then_inc(s_xsh, 1)
            act.wait_ge(s_rdiff, 1)
            nc.scalar.activation(g4[0][:, :, :], g4[0][:, :, :], ACT.Exp).then_inc(s_rexp, 1)
            act.wait_ge(s_rdiff, 2)
            nc.scalar.activation(b4[4][:, :], b4[4][:, :], ACT.Exp).then_inc(s_rexp, 1)

            act.wait_ge(s_rounds, 1)
            rounds = act.value_load(rounds_i[0:1, 0:1], min_val=1, max_val=T // SLOT)
            act.wait_ge(s_xsl, NB)
            with act.Fori(0, rounds) as r:
                with act.Fori(0, BODIES) as i:
                    n = r * BODIES + i
                    act.wait_ge(s_pwm, n + 1)
                    for s in range(2):
                        for j in range(2):
                            rows = slice(j * SLOT, (j + 1) * SLOT)
                            last = nc.scalar.activation(pair_w[s][rows, :], tiles[W_BANK][rows, 2 * s + j:2 * s + j + 1],
                                                        ACT.Copy)
                    last.then_inc(s_pw, 1)
                    for s in range(2):
                        act.wait_ge(s_gu[s], n + 1)
                        nc.scalar.activation(hs[s][:, :], tiles[GU_BANK[s]][:, 0:FF], ACT.Silu).then_inc(s_silu[s], 1)

                    def hidden_out(s):
                        act.wait_ge(s_hTm[s], n + 1)
                        nc.scalar.activation(hT[s][:, :, :].rearrange("p f t -> p (f t)"),
                                             tiles[H_BANK[s]][:, 0:2 * P], ACT.Copy).then_inc(s_hT[s], 1)

                    hidden_out(0)
                    for s in range(2):
                        act.wait_ge(s_ohTm[s], n + 1)
                        nc.scalar.activation(onehotT[s][:, :, :].rearrange("p b t -> p (b t)"), tiles[OH_BANK[s]][:, :],
                                             ACT.Copy).then_inc(s_ohT[s], 1)
                    hidden_out(1)
                    for s in range(2):
                        act.wait_ge(s_down[s], n + 1)
                        for half in range(2):
                            last = nc.scalar.activation(y_hi[s][:, half * 512:(half + 1) * 512],
                                                        tiles[DOWN_BANKS[s][half]][:, :], ACT.Copy)
                        last.then_inc(s_yhi[s], 1)
                    for u in (6, 7, 14, 15):
                        act.wait_ge(s_sc[u % 4], 4 * n + u // 4 + 1)
                        act.wait_ge(s_padd[u % 2], 2 * n + u // 8 + 1)
                        nc.scalar.activation(sums[u % 2][:, :], tiles[SCATTER_BANKS[u % 4]][:, :], ACT.Copy)\
                            .then_inc(s_add[u % 4], 1)

        @block.vector
        def _(dve):
            link = chain(dve, s_dve)
            norms = [0]

            def norm_mean(src, rows, groups, width):
                norms[0] += 1
                c0 = 8 * (norms[0] % 2)
                mean = stat[0:rows, c0:c0 + groups]
                dve.wait_ge(s_square, norms[0])
                if norms[0] > 2:
                    dve.wait_ge(s_norm, norms[0] - 2)
                link(nc.vector.tensor_reduce(mean, src, AX.X, ALU.add))
                nc.vector.tensor_scalar(mean, mean, 1.0 / width, EPS,
                                        ALU.mult, ALU.add).then_inc(s_mean2, 1)

            nc.vector.memset(stat[:, :], 1.0).then_inc(s_set, 1)
            nc.vector.memset(ones[:, :], 1.0).then_inc(s_ones, 1)
            nc.vector.memset(minus_half[:, :], -0.5).then_inc(s_set, 1)
            for step in SCHEDULE:
                kind = step[0]
                if kind == "prep":
                    c = step[1]
                    dve.wait_ge(s_hi, c + 1)
                    nc.vector.tensor_tensor(w_view(wlo[c % 2], c), w_view(wraw[c % 2], c),
                                            w_view(whi[c % 2], c).bitcast(F32), ALU.subtract).then_inc(s_lo, 1)
                elif kind == "xT":
                    dve.wait_ge(s_sumsq, NB + 1)
                    nc.vector.tensor_scalar(stat[:, 0:NB + 1], stat[:, 0:NB + 1], 1.0 / D, EPS,
                                            ALU.mult, ALU.add).then_inc(s_mean, 1)
                    dve.wait_ge(s_rstd, 1)
                    for b in range(NB):
                        nc.vector.tensor_scalar(xr[:, b, :], h[:, b, :], rstd[:, b:b + 1], None, ALU.mult).then_inc(s_xr, 1)
                    nc.vector.tensor_scalar(xm[:, :], xm[:, :], rstd[0:NM, NB:NB + 1], None, ALU.mult).then_inc(s_xr, 1)
                    dve.wait_ge(s_early, EARLY_DMAS * 16)
                    for k in range(KT):
                        dve.wait_ge(s_xhi, k + 1)
                        nc.vector.scalar_tensor_tensor(xlo[:, k, NM:XC], banks.get(("xT", k))[:, :], norm1[:, k:k + 1],
                                                       xhi[:, k, NM:XC].bitcast(F32), ALU.mult, ALU.subtract)\
                            .then_inc(banks.read(("xT", k)), 1)
                    dve.wait_ge(*banks.filled("xmT"))
                    ps = banks.get("xmT")[:, 0:KT * NM].rearrange("p (k m) -> p k m", k=KT)
                    nc.vector.tensor_tensor(xmf[:, :, :], ps, norm1[:, :].unsqueeze(2).to_broadcast([P, KT, NM]),
                                            ALU.mult).then_inc(banks.read("xmT"), 1)
                    dve.wait_ge(s_xhi, KT + 1)
                    nc.vector.tensor_tensor(xlo[:, :, 0:NM], xmf[:, :, :], xhi[:, :, 0:NM].bitcast(F32),
                                            ALU.subtract).then_inc(s_xlo, 1)
                elif kind == "unit":
                    _, c, u = step
                    name, c0, n, kt = CHUNKS[c]
                    if name == "vg" and c == 4:
                        dve.wait_ge(*banks.filled(step))
                        dst = vgm[:, CW:2 * CW] if u == "m" else vg[:, u, CW:2 * CW]
                        nc.vector.tensor_copy(dst, banks.get(step)[0:NM if u == "m" else P, 0:CW]).then_inc(banks.read(step), 1)
                    elif name == "qa" and c == 7:
                        dve.wait_ge(*banks.filled(step))
                        nc.vector.tensor_copy(q_heads(u, 1), banks.get(step)[:, 0:CW].rearrange("p (i d) -> p i d", d=DH)).then_inc(banks.read(step), 1)
                    elif name == "rg":
                        dve.wait_ge(s_re, (c - 8) * NB + u + 1)
                        r = rgs[:, u, (c - 8) * CW:(c - 7) * CW]
                        link(nc.vector.tensor_scalar(r, r, 1.0, None, ALU.add))
                        link(nc.vector.reciprocal(r, r))
                        nc.vector.tensor_tensor(r, banks.get(step)[:, 0:CW], r, ALU.mult).then_inc(banks.read(step), 1)
                    elif name in ("wa", "wg"):
                        j = c0 // P + u
                        t = (sig_a if name == "wa" else sig_g)[:, j, :]
                        dve.wait_ge(s_sig, 16)
                        dve.wait_ge(*banks.filled(step))
                        nc.vector.tensor_tensor(t, banks.get(step)[:, :], t, ALU.mult).then_inc(banks.read(step), 1)
                        if name == "wa":
                            dve.wait_ge(*banks.emptied(step))
                            dve.wait_ge(*banks.emptied(("unit", c - 1, u)))
                            nc.vector.tensor_tensor(t, t, sig_g[:, j, :], ALU.add).then_inc(s_mer, 1)
                            dve.wait_ge(s_mhi, j + 1)
                            nc.vector.tensor_tensor(mlo[:, j, :], t, mhi[:, j, :].bitcast(F32), ALU.subtract).then_inc(s_mlo, 1)
                    elif name == "wo":
                        dve.wait_ge(*banks.filled(step))
                        nc.vector.tensor_tensor(h[:, u, c0:c0 + n], banks.get(step)[:, 0:n], h[:, u, c0:c0 + n],
                                                ALU.add).then_inc(banks.read(step), 1)
                elif kind == "z":
                    dve.wait_ge(s_const, (CONST_DMAS - EARLY_DMAS) * 16)
                    nc.vector.tensor_scalar(nsinks[:, :], sinks[:, :], -1.0, None, ALU.mult).then_inc(s_set, 1)
                    for j in range(2):
                        dve.wait_ge(*banks.filled(("z", j)))
                        ps = banks.get(("z", j))
                        link(nc.vector.tensor_single_scalar(g_q3[:, j, :], ps[:, :], 0.0, ALU.min))
                        nc.vector.scalar_tensor_tensor(g_d[:, j, :], g_q3[:, j, :], -2.0, ps[:, :], ALU.mult, ALU.add)\
                            .then_inc(banks.read(("z", j)), 1)
                    dve.wait_ge(*banks.filled("zm"))
                    ps = banks.get("zm")[:, 0:2 * NM]
                    zf, bf = (t[:, :, :].rearrange("p j m -> p (j m)") for t in (zm, bm))
                    link(nc.vector.tensor_single_scalar(bf, ps, 0.0, ALU.min))
                    nc.vector.scalar_tensor_tensor(zf, bf, -2.0, ps, ALU.mult, ALU.add).then_inc(banks.read("zm"), 1)
                    for j in range(2):
                        dve.wait_ge(s_l, j + 1)
                        dve.wait_ge(*banks.emptied(("z", j)))
                        link(nc.vector.tensor_tensor(g_q3[:, j, :], g_q3[:, j, :], g_l[:, j, :], ALU.subtract))
                        dve.wait_ge(s_reset, 2)
                        link(nc.vector.tensor_tensor_scan(g_b[:, j, :], reset[:, :], g_q3[:, j, :], 0.0, ALU.mult, ALU.add))
                    dve.wait_ge(s_l, 3)
                    dve.wait_ge(*banks.emptied("zm"))
                    link(nc.vector.tensor_tensor(bm[:, :, :], bm[:, :, :], lm[:, :, :], ALU.subtract))
                    for j in range(2):
                        link(nc.vector.tensor_tensor_scan(zm[:, j, :], ones[:, 0:NM], bm[:, j, :], 0.0, ALU.mult, ALU.add))
                    bv, dv, k4 = chunks_of(g_b), chunks_of(g_d), chunks_of(g_k4)
                    full = [P, 2 * NCH, GC]
                    nc.vector.tensor_tensor(dv, bv, bv[:, :, GC // 2:GC // 2 + 1].to_broadcast(full), ALU.subtract).then_inc(s_diff, 1)
                    nc.vector.tensor_tensor(k4, bv[:, :, GC - 1:GC].to_broadcast(full), bv, ALU.subtract).then_inc(s_diff, 1)
                    nc.vector.tensor_tensor(lm[:, :, :], zm[:, :, NM - 1:NM].to_broadcast([P, 2, NM]), zm[:, :, :],
                                            ALU.subtract).then_inc(s_diff, 1)
                elif kind == "decay":
                    for j in range(2):
                        dve.wait_ge(*banks.emptied(("unit", 1, j)))
                        dve.wait_ge(*banks.emptied(("unit", 2, j)))
                    dve.wait_ge(*banks.emptied(("unit", 2, "m")))
                    for i, (t, o) in enumerate(((g_q1, g_q), (g_k1, g_k), (g_q3, g_q), (g_k4, g_k), (kgm, lm))):
                        dve.wait_ge(s_exp, i + 1)
                        nc.vector.tensor_tensor(t[:, :, :], t[:, :, :], o[:, :, :], ALU.mult).then_inc(s_gla_in, 1)
                elif kind == "kdm":
                    dve.wait_ge(*banks.filled("kdm"))
                    nc.vector.tensor_copy(kdm[:, :], banks.get("kdm")[0:NM, 0:CW]).then_inc(banks.read("kdm"), 1)
                elif kind == "kd":
                    dve.wait_ge(*banks.filled(step))
                    nc.vector.tensor_copy(kd[:, step[1], :], banks.get(step)[:, 0:CW]).then_inc(banks.read(step), 1)
                elif kind == "kv":
                    c = step[1]
                    dve.wait_ge(*banks.filled(step))
                    ps = banks.get(step)
                    if c < 0:
                        nc.vector.tensor_copy(st[:, 0, :, :], ps[:, 0:2 * GV].rearrange("p (j v) -> p j v", j=2))\
                            .then_inc(banks.read(step), 1)
                    else:
                        dve.wait_ge(s_exp, 6)
                        dve.wait_ge(*banks.emptied(("kv", c - 1)))
                        for j in range(2):
                            last = nc.vector.scalar_tensor_tensor(st[:, c + 1, j, :], st[:, c, j, :],
                                                                  dec[:, j * NCH + c:j * NCH + c + 1],
                                                                  ps[:, j * GV:(j + 1) * GV], ALU.mult, ALU.add)
                        last.then_inc(banks.read(step), 1)
                elif kind == "sig":
                    _, c, u = step
                    j = (c - 10) // 2 * 2 + u
                    t = (sig_a if CHUNKS[c][0] == "ga" else sig_g)[:, j, :]
                    dve.wait_ge(*banks.emptied(("unit", c, u)))
                    link(nc.vector.tensor_scalar(t, t, 1.0, None, ALU.add))
                    nc.vector.reciprocal(t, t).then_inc(s_sig, 1)
                elif kind == "krope":
                    norm_mean(n_sq[:, :].rearrange("p (g d) -> p g d", d=DH), P, 8, DH)
                    norm_mean(n_sq[0:NM, 0:P].rearrange("p (g d) -> p g d", d=DH), NM, HKV, DH)
                elif kind == "qrope":
                    norm_mean(n_sq[:, :].rearrange("p (g d) -> p g d", d=DH), P, HQ, DH)
                elif kind == "ognorm":
                    norm_mean(n_sq[:, :].rearrange("p (g d) -> p g d", d=GV), P, GH, GV)
                elif kind == "S":
                    _, b, i = step
                    if (b, i) == (0, 0):
                        dve.wait_ge(s_qrope, NB)
                    for j in range(2):
                        n = 2 * (4 * b + i) + j
                        hd = j * 4 + i
                        name = ("S", b, i, j)
                        st_ = att_stat[:, b % 2, :, hd:hd + 1]
                        c0 = 128 if b == 0 else 0
                        dve.wait_ge(*banks.filled(name))
                        if n >= 4:
                            dve.wait_ge(*banks.filled(("PT",) + head_before(n, 4)))
                        nc.vector.tensor_tensor_reduce(out=prob[n % 4][:, c0:272], in0=banks.get(name)[:, c0:272],
                                                       in1=C("mask")[:, c0:272], scale=1.0, scalar=-3.0e38,
                                                       op0=ALU.add, op1=ALU.max, accum_out=st_[:, 0, :])\
                            .then_inc(banks.read(name), 1)
                        dve.wait_ge(*banks.emptied(name))
                        nc.vector.tensor_scalar(st_[:, 1, :], st_[:, 0, :], -SCALE, nsinks[:, hd:hd + 1],
                                                ALU.mult, ALU.min).then_inc(s_max, 1)
                elif kind == "PT":
                    _, b, i = step
                    name = ("PT", b, i, 1)
                    dve.wait_ge(*banks.filled(name))
                    if 4 * b + i:
                        dve.wait_ge(s_pv, 4 * b + i)
                    ps = banks.get(name)
                    c0 = 128 if b == 0 else 0
                    nc.vector.tensor_copy(pt[1][:, c0:256], ps[:, c0:256])
                    nc.vector.tensor_copy(ptm[1][:, :], ps[0:NM, 256:384]).then_inc(banks.read(name), 1)
                elif kind == "onorm":
                    b = step[1]
                    st_ = att_stat[:, b % 2, :, :]
                    dve.wait_ge(s_es, 8 * (b + 1))
                    link(nc.vector.tensor_tensor(st_[:, 4, :], st_[:, 2, :], st_[:, 3, :], ALU.add))
                    link(nc.vector.reciprocal(st_[:, 4, :], st_[:, 4, :]))
                    dve.wait_ge(s_pv, 4 * (b + 1))
                    if b:
                        dve.wait_ge(*banks.filled(("oT", b - 1)))
                    nc.vector.tensor_tensor(o_tok[:, :].rearrange("p (h d) -> p h d", d=DH),
                                            banks.get(("PV", b))[:, :].rearrange("p (h d) -> p h d", d=DH),
                                            st_[:, 4, :].unsqueeze(2).to_broadcast([P, HQ, DH]), ALU.mult)\
                        .then_inc(banks.read(("PV", b)), 1)
                elif kind in ("oT", "ogT"):
                    b = step[1]
                    dst, hi, s = (olo, ohi, s_ohi) if kind == "oT" else (oglo, oghi, s_oghi)
                    dve.wait_ge(s, b + 1)
                    if kind == "ogT" and b == 0:
                        dve.wait_ge(s_ogn, NB)
                    cb = slice(b * P, (b + 1) * P)
                    nc.vector.tensor_tensor(dst[:, :, cb], banks.get(step)[:, :].rearrange("p (j t) -> p j t", j=4),
                                            hi[:, :, cb].bitcast(F32), ALU.subtract).then_inc(banks.read(step), 1)

            def tt(o, a, b, op):
                return link(nc.vector.tensor_tensor(o, a, b, op))

            dve.wait_ge(s_sq2, NB)
            nc.vector.tensor_scalar(stat[:, 0:NB], stat[:, 0:NB], 1.0 / D, EPS, ALU.mult, ALU.add).then_inc(s_m2, 1)
            dve.wait_ge(s_r2, 1)
            for b in range(NB):
                nc.vector.tensor_scalar(xs[:, b, :], h[:, b, :], rstd[:, b:b + 1], None, ALU.mult).then_inc(s_xs_loc, 1)
            for b in range(NB):
                for half in range(2):
                    name = ("nT", b, half)
                    dve.wait_ge(*banks.filled(name))
                    nc.vector.tensor_tensor(xnT[:, 4 * half:4 * half + 4, b * P:(b + 1) * P],
                                            banks.get(name)[:, :].rearrange("p (k t) -> p k t", k=4),
                                            norm2[:, 4 * half:4 * half + 4].unsqueeze(2).to_broadcast([P, 4, P]),
                                            ALU.mult).then_inc(banks.read(name), 1)
                dve.wait_ge(s_xsh, b + 1)
                nc.vector.tensor_tensor(xs_lo[:, b, :], xs[:, b, :], xs_hi[:, b, :].bitcast(F32),
                                        ALU.subtract).then_inc(s_xsl, 1)
                dve.wait_ge(*banks.filled(("logit", b)))
                nc.vector.tensor_copy(logits[:, b, :], banks.get(("logit", b))[:, 0:NG + NE]).then_inc(banks.read(("logit", b)), 1)
            for b in (2, 3):
                dve.wait_ge(*banks.emptied(("logit", b)))

            def bc(t, shape, axis=2):
                return t.unsqueeze(axis).to_broadcast(shape)

            def first_max(v, onehot, maxv, tmp, idx, numbers, n):
                full = [P, NB, n]
                link(nc.vector.tensor_reduce(maxv, v, AX.X, ALU.max))
                tt(tmp, v, bc(maxv, full), ALU.is_lt)
                link(nc.vector.scalar_tensor_tensor(tmp, tmp, 1000.0, bc(numbers, full, 1), ALU.mult, ALU.add))
                link(nc.vector.tensor_reduce(idx, tmp, AX.X, ALU.min))
                tt(onehot, bc(numbers, full, 1), bc(idx, full), ALU.is_equal)

            gl = logits[:, :, 0:NG]
            group, g_tmp = g4[1][:, :, :], g4[2][:, :, :]
            gmax, gw, v1, v2, p2, p1, idx, rec = (b4[i][:, :] for i in (0, 1, 2, 3, 4, 5, 6, 7))
            first_max(gl, group, gmax, g_tmp, idx, C("gi"), NG)
            nc.vector.tensor_tensor(g4[0][:, :, :], gl, bc(gmax, [P, NB, NG]), ALU.subtract).then_inc(s_rdiff, 1)
            el = logits[:, :, NG:NG + NE].rearrange("p b (g e) -> p b g e", g=NG)
            four = [P, NB, NG, EPG]
            sel = r_tmp[:, :, :].rearrange("p b (g e) -> p b g e", g=NG)
            tt(sel, el, bc(group, four, 3), ALU.mult)
            ev, ev2, one1, one2, e_tmp = (t[:, :, :] for t in e8[0:5])
            link(nc.vector.tensor_reduce(ev, sel.rearrange("p b g e -> p b e g"), AX.X, ALU.add))
            first_max(ev, one1, v1, e_tmp, idx, C("ei"), EPG)
            link(nc.vector.scalar_tensor_tensor(ev2, one1, -3.0e38, ev, ALU.mult, ALU.add))
            first_max(ev2, one2, v2, e_tmp, idx, C("ei"), EPG)
            nc.vector.tensor_tensor(b4[4][:, :], v2, v1, ALU.subtract).then_inc(s_rdiff, 1)
            for one, dst in ((one1, first_e), (one2, second_e)):
                tt(dst[:, :, :].rearrange("p b (g e) -> p b g e", g=NG), bc(one, four, 2), bc(group, four, 3), ALU.mult)
            nc.vector.tensor_tensor(chosen[:, :, :], first_e[:, :, :], second_e[:, :, :], ALU.add).then_inc(s_choice, 1)
            dve.wait_ge(s_rexp, 2)
            link(nc.vector.tensor_reduce(gw, g4[0][:, :, :], AX.X, ALU.add))
            link(nc.vector.tensor_scalar(rec, p2, 1.0, None, ALU.add))
            tt(rec, rec, gw, ALU.mult)
            link(nc.vector.reciprocal(p1, rec))
            tt(p2, p2, p1, ALU.mult)
            all_e = [P, NB, NE]
            tt(r_tmp[:, :, :], first_e[:, :, :], bc(p1, all_e), ALU.mult)
            tt(r_sel[:, :, :], second_e[:, :, :], bc(p2, all_e), ALU.mult)
            tt(token_w[:, :, :], r_tmp[:, :, :], r_sel[:, :, :], ALU.add)
            dve.wait_ge(*banks.filled("rank"))
            ps = banks.get("rank")
            link(nc.vector.tensor_copy(rank[:, :, 0:NE], ps[:, 0:NB * NE].rearrange("p (b e) -> p b e", e=NE)))
            link(nc.vector.memset(rank[:, :, NE:], -1.0))
            nc.vector.tensor_copy(counts[:, :], ps[:, NB * NE:(NB + 1) * NE]).then_inc(banks.read("rank"), 1)
            dve.wait_ge(*banks.emptied("rank"))
            link(nc.vector.tensor_reduce(n_round[:, 0:1], counts[:, :], AX.X, ALU.max))
            link(nc.vector.tensor_scalar(e8[5][:, 0, :], C("slots")[:, 0:T // SLOT], float(SLOT), n_round[:, 0:1],
                                         ALU.mult, ALU.is_lt))
            link(nc.vector.tensor_reduce(n_round[:, 1:2], e8[5][:, 0, :], AX.X, ALU.add))
            nc.vector.tensor_copy(rounds_i[:, :], n_round[:, 1:2]).then_inc(s_rounds, 1)
            link(nc.vector.scalar_tensor_tensor(rank[:, :, 0:NE], rank[:, :, 0:NE], 1.0, chosen[:, :, :], ALU.add, ALU.mult))
            link(nc.vector.tensor_scalar(rank[:, :, 0:NE], rank[:, :, 0:NE], -1.0, None, ALU.add))

            dve.wait_ge(s_rounds, 1)
            rounds = dve.value_load(rounds_i[0:1, 0:1], min_val=1, max_val=T // SLOT)
            dve.wait_ge(s_xsl, NB)
            with dve.Fori(0, rounds) as r:
                def build_onehots(e):
                    full = [P, NB, 4, SLOT]
                    ranks = rank[:, :, 0:4] if e is None else rank[:, :, bass.ds(e, 4)]
                    nc.vector.tensor_tensor(onehot[:, :, :].rearrange("p b (e t) -> p b e t", e=4),
                                            C("slots").unsqueeze(1).unsqueeze(1).to_broadcast(full),
                                            ranks.unsqueeze(3).to_broadcast(full), ALU.is_equal).then_inc(s_oh, 1)

                dve.wait_ge(s_rank, r + 1)
                build_onehots(None)
                with dve.Fori(0, BODIES) as i:
                    n = r * BODIES + i
                    dve.wait_ge(s_oh, r * (BODIES + 1) + i + 1)
                    for g, bank in enumerate(GATHER_BANKS):
                        dve.wait_ge(s_xg[g], n + 1)
                        nc.vector.tensor_tensor(xgT[:, 2 * g:2 * g + 2, :], tiles[bank][:, :].rearrange("p (k t) -> p k t", k=2),
                                                bc(norm2[:, 2 * g:2 * g + 2], [P, 2, 2 * P]), ALU.mult).then_inc(s_xgT[g], 1)
                    dve.wait_ge(s_pw, n + 1)
                    for s in range(2):
                        dve.wait_ge(s_silu[s], n + 1)
                        nc.vector.scalar_tensor_tensor(hg[s][:, :], tiles[GU_BANK[s]][:, FF:2 * FF], pair_w[s][:, 0:1],
                                                       hs[s][:, :], ALU.mult, ALU.mult).then_inc(s_hg[s], 1)
                    for s in range(2):
                        dve.wait_ge(s_ohTm[s], n + 1)
                    nc.vector.tensor_tensor(waited[:, :], norm2[:, 0:1], norm2[:, 0:1], ALU.add)
                    build_onehots(4 * i + 4)
                    for s in range(2):
                        dve.wait_ge(s_yhi[s], n + 1)
                        for half in range(2):
                            cols_ = slice(half * 512, (half + 1) * 512)
                            last = nc.vector.tensor_tensor(y_lo[s][:, cols_], tiles[DOWN_BANKS[s][half]][:, :],
                                                           y_hi[s][:, cols_].bitcast(F32), ALU.subtract)
                        last.then_inc(s_ylo[s], 1)
                    for u in range(16):
                        b, half = u % 8 // 2, u % 2
                        if b == NB - 1:
                            continue
                        cols_ = slice(half * 512, (half + 1) * 512)
                        dve.wait_ge(s_sc[u % 4], 4 * n + u // 4 + 1)
                        if u % 8 == 0:
                            dve.wait_ge(s_add[1], 4 * n + u // 4 + 1)
                        nc.vector.tensor_tensor(h[:, b, cols_], h[:, b, cols_], tiles[SCATTER_BANKS[u % 4]][:, :],
                                                ALU.add).then_inc(s_add[u % 4], 1)
                nc.vector.tensor_scalar(rank[:, :, :], rank[:, :, :], -float(SLOT), None, ALU.add).then_inc(s_rank, 1)

        @block.gpsimd
        def _(pool):
            link = chain(pool, s_pool)
            norms = [0]

            def tt(o, a, b, op=ALU.mult):
                return nc.gpsimd.tensor_tensor(o, a, b, op)

            def rms(rows, groups):
                norms[0] += 1
                c0 = 8 * (norms[0] % 2)
                pool.wait_ge(s_mean2, norms[0])
                tt(rstd[0:rows, 0:groups], stat[0:rows, c0:c0 + groups], minus_half[0:rows, 0:groups], ALU.pow)\
                    .then_inc(s_norm, 1)
                pool.wait_ge(s_norm, norms[0])

            def rope(x_, cosw, sinw, xn, t, dst, rows, groups, done, count):
                hh = DH // 2
                rms(rows, groups)
                link(tt(xn, x_, rstd[0:rows, 0:groups].unsqueeze(2).to_broadcast([rows, groups, DH])))
                tt(t[:, :, 0:hh], xn[:, :, hh:DH], sinw[:, :, 0:hh])
                link(tt(t[:, :, hh:DH], xn[:, :, 0:hh], sinw[:, :, hh:DH]))
                link(tt(xn, xn, cosw))
                tt(dst, xn, t, ALU.add).then_inc(done, 1)
                pool.wait_ge(done, count)

            nc.gpsimd.memset(gdT[:, :], 1.0).then_inc(s_set2, 1)
            nc.gpsimd.memset(reset[:, :], 1.0).then_inc(s_reset, 1)
            pool.wait_ge(s_reset, 1)
            nc.gpsimd.memset(reset[:, 0:T:GC], 0.0).then_inc(s_reset, 1)
            for step in SCHEDULE:
                kind = step[0]
                if kind == "xT":
                    pool.wait_ge(s_set, 2)
                    pool.wait_ge(s_mean, 1)
                    tt(rstd[:, 0:NB + 1], stat[:, 0:NB + 1], minus_half[:, 0:NB + 1], ALU.pow).then_inc(s_rstd, 1)
                    pool.wait_ge(s_early, EARLY_DMAS * 16)
                    pool.wait_ge(s_const, (CONST_DMAS - EARLY_DMAS) * 16)
                    for i, (t, w) in enumerate((("cc", 0), ("ss", 1), ("cc", 2), ("ss", 3))):
                        tt(tab[:, i, :, :], C(t).rearrange("p (b d) -> p b d", d=DH),
                           qk_w[:, w:w + 1, :].to_broadcast([P, NB, DH]))
                    tt(tabm[:, 0, :], C("ccm", NM), qk_w[0:NM, 2, :])
                    link(tt(tabm[:, 1, :], C("ssm", NM), qk_w[0:NM, 3, :]))
                elif kind == "kdm":
                    pool.wait_ge(s_gla_in, 5)
                    for t in att:
                        nc.gpsimd.memset(t[:, :, :], 0.0).then_inc(s_zero, 1)
                elif kind == "krope":
                    for b in range(NB):
                        pool.wait_ge(*banks.emptied(("unit", 5, b)))
                    pool.wait_ge(*banks.emptied(("unit", 5, "m")))
                    v = k_tok[:, :, :].rearrange("p b (g d) -> p (b g) d", d=DH)
                    rms(P, 8)
                    xn, t = view(n_x, P, 8), view(n_t, P, 8)
                    link(tt(xn, v, rstd[:, 0:8].unsqueeze(2).to_broadcast([P, 8, DH])))
                    hh = DH // 2
                    for g in range(HKV):
                        xh, th = (u.rearrange("p (b g) d -> p b g d", g=HKV)[:, :, g, :] for u in (xn, t))
                        tt(th[:, :, 0:hh], xh[:, :, hh:DH], tab[:, 3, :, 0:hh])
                        link(tt(th[:, :, hh:DH], xh[:, :, 0:hh], tab[:, 3, :, hh:DH]))
                        link(tt(xh, xh, tab[:, 2, :, :]))
                    tt(v, xn, t, ALU.add).then_inc(s_krope, 1)
                    pool.wait_ge(s_krope, 1)
                    m = km[:, 0:P].rearrange("p (g d) -> p g d", d=DH)
                    rope(m, tabm[:, 0:1, :].to_broadcast([NM, HKV, DH]), tabm[:, 1:2, :].to_broadcast([NM, HKV, DH]),
                         view(n_x, NM, HKV), view(n_t, NM, HKV), krm[:, :].rearrange("p (g d) -> p g d", d=DH),
                         NM, HKV, s_krope, 2)
                elif kind == "qrope":
                    b = step[1]
                    pool.wait_ge(*banks.emptied(("unit", 6, b)))
                    pool.wait_ge(*banks.emptied(("unit", 7, b)))
                    q = q_tok[:, b, :].rearrange("p (g d) -> p g d", d=DH)
                    rope(q, tab[:, 0, b:b + 1, :].to_broadcast([P, HQ, DH]), tab[:, 1, b:b + 1, :].to_broadcast([P, HQ, DH]),
                         view(n_x, P, HQ), view(n_t, P, HQ), q, P, HQ, s_qrope, b + 1)
                elif kind == "attT":
                    b = step[1]
                    pool.wait_ge(*banks.emptied(step))
                    nc.gpsimd.affine_select(out=att[b % 2][:, :, :], in_=att[b % 2][:, :, :], compare_op=ALU.is_ge,
                                            fill=0.0, base=0, pattern=[[0, GH], [1, P]], channel_multiplier=-1)\
                        .then_inc(s_attm, 1)
                elif kind == "unit" and CHUNKS[step[1]][0] == "rg":
                    _, c, u = step
                    pool.wait_ge(*banks.emptied(step))
                    r = rgs[:, u, (c - 8) * CW:(c - 7) * CW].rearrange("p (h v) -> p h v", v=GV)
                    link(tt(r, r, gla_w[:, :].unsqueeze(1).to_broadcast([P, 2, GV])))
                elif kind == "ognorm":
                    b = step[1]
                    pool.wait_ge(*banks.emptied(("glao", b)))
                    o = og[b][:, :].rearrange("p (h v) -> p h v", v=GV)
                    rms(P, GH)
                    link(tt(o, o, rstd[:, 0:GH].unsqueeze(2).to_broadcast([P, GH, GV])))
                    tt(rgs[:, b, :], og[b][:, :], rgs[:, b, :]).then_inc(s_ogn, 1)
            pool.wait_ge(s_m2, 1)
            tt(rstd[:, 0:NB], stat[:, 0:NB], minus_half[:, 0:NB], ALU.pow).then_inc(s_r2, 1)
            pool.wait_ge(s_rounds, 1)
            rounds = pool.value_load(rounds_i[0:1, 0:1], min_val=1, max_val=T // SLOT)
            with pool.Fori(0, rounds) as r:
                with pool.Fori(0, BODIES) as i:
                    n = r * BODIES + i
                    for u in (6, 7, 14, 15):
                        cols_ = slice(u % 2 * 512, (u % 2 + 1) * 512)
                        pool.wait_ge(s_add[u % 4], 4 * n + u // 4 + 2)
                        pool.wait_ge(s_padd[u % 2], 2 * n + u // 8 + 1)
                        tt(h[:, NB - 1, cols_], h[:, NB - 1, cols_], sums[u % 2][:, :], ALU.add).then_inc(s_padd[u % 2], 1)


_INS = ["x", "meta_tokens", "norm1_w", "w_in", "q_norm_w", "k_norm_w", "attn_sinks", "gla_gate_up", "gla_gate_bias",
        "gla_norm_w", "w_attn_branch", "w_gla_branch", "w_out", "norm2_w", "router_group", "router_expert",
        "expert_w_gate", "expert_w_up", "expert_w_down"]


def kernel(**inputs):
    import concourse.bacc as bacc
    from concourse.bass_utils import run_bass_kernel_spmd

    nc = bacc.Bacc("TRN2", target_bir_lowering=False, num_devices=1)
    arrays, args = {}, []
    for name in _INS:
        a = np.ascontiguousarray(inputs[name])
        arrays[f"in_{name}"] = a
        args.append(nc.dram_tensor(f"in_{name}", a.shape, mybir.dt.from_np(a.dtype), kind="ExternalInput").ap())
    table = shape_tables()
    arrays["table"] = table
    args.append(nc.dram_tensor("table", table.shape, F32, kind="ExternalInput").ap())
    args.append(nc.dram_tensor("out", (1, T, D), F32, kind="ExternalOutput").ap())
    layer_kernel(nc, *args)
    r = run_bass_kernel_spmd(nc, [arrays], core_ids=[0])
    return r.results[0]["out"]
```
